# Optimizing a Trainium2 kernel written in Bass

```python
import jax, jax.numpy as jnp
from jax import lax
import numpy as np
import math

D_MODEL = 1024
BATCH = 1
SEQ = 512
DEPTH = 2

CHUNK = 64
N_MIXERS = 2
HEAD_SIZE = 64
N_HEADS = D_MODEL // HEAD_SIZE
D_FF = 4 * D_MODEL
CONV_WIDTH = 3
D_DECAY_LORA = 64
D_AAA_LORA = 64
D_MV_LORA = 32
D_GATE_LORA = 160
N_CONV_LAYERS = (DEPTH + 1) // 2
N_RWKV_LAYERS = DEPTH // 2
N_VRES = max(N_RWKV_LAYERS - 1, 0)
N_MOD = 6
NORM_EPS = 1e-6
GN_EPS = 64e-5


def _rmsnorm(x, g):
    x32 = x.astype(jnp.float32)
    y = x32 * lax.rsqrt(jnp.mean(x32 * x32, axis=-1, keepdims=True) + NORM_EPS)
    return (y * g.astype(jnp.float32)).astype(x.dtype)

def _modulate(h, shift, scale):
    return h * (1 + scale[:, None, :]) + shift[:, None, :]

def _short_conv_mixer(h, w_in, conv_w, w_out):
    bch = h @ w_in
    b_gate, c_gate, hv = jnp.split(bch, 3, axis=-1)
    u = c_gate * hv
    conv = lax.conv_general_dilated(
        u, conv_w[:, None, :], window_strides=(1,),
        padding=[(CONV_WIDTH - 1, 0)],
        dimension_numbers=('NWC', 'WIO', 'NWC'),
        feature_group_count=D_MODEL)
    return (b_gate * conv) @ w_out

def _wkv7_scan(r, w, k, v, a, b):
    bsz, seq = r.shape[0], r.shape[1]

    def to_chunks(t):
        return t.transpose(1, 0, 2, 3).reshape(seq // CHUNK, CHUNK, bsz, N_HEADS, HEAD_SIZE)

    def frame_step(state, inp):
        r_t, w_t, k_t, v_t, a_t, b_t = inp
        sa = jnp.einsum('bhvk,bhk->bhv', state, a_t)
        state = (state * w_t[:, :, None, :]
                 + sa[..., None] * b_t[:, :, None, :]
                 + v_t[..., None] * k_t[:, :, None, :])
        y_t = jnp.einsum('bhvk,bhk->bhv', state, r_t)
        return state, y_t

    def chunk_step(state, inp_chunk):
        return lax.scan(frame_step, state, inp_chunk)

    s0 = jnp.zeros((bsz, N_HEADS, HEAD_SIZE, HEAD_SIZE), jnp.float32)
    inputs = (to_chunks(r), to_chunks(w), to_chunks(k), to_chunks(v), to_chunks(a), to_chunks(b))
    _, y = lax.scan(chunk_step, s0, inputs)
    return y.reshape(seq, bsz, N_HEADS, HEAD_SIZE).transpose(1, 0, 2, 3)

def _rwkv7_mixer(h, v_first, vres, mu, w_rkv, w_o, w0, w1, w2, a0, a1, a2,
                 g1, g2, k_k, k_a, r_k, ln_w, ln_b):
    bsz, seq, d = h.shape
    h_prev = jnp.pad(h, ((0, 0), (1, 0), (0, 0)))[:, :-1]
    xx = h_prev - h
    xr, xw, xk, xv, xa, xg = h[None] + xx[None] * mu[:, None, None, :]
    r, k, v = jnp.einsum('nbsd,nde->nbse', jnp.stack([xr, xk, xv]), w_rkv)
    w = -jax.nn.softplus(-(w0 + jnp.tanh(xw @ w1) @ w2)) - 0.5
    a = jax.nn.sigmoid(a0 + (xa @ a1) @ a2)
    g = jax.nn.sigmoid(xg @ g1) @ g2
    if vres is None:
        v_first = v
    else:
        v0, v1, v2 = vres
        v = v + (v_first - v) * jax.nn.sigmoid(v0 + (xv @ v1) @ v2)

    def heads(t):
        return t.reshape(bsz, seq, N_HEADS, HEAD_SIZE).astype(jnp.float32)

    kk = heads(k * k_k)
    kk = kk / jnp.maximum(jnp.sqrt(jnp.sum(kk * kk, axis=-1, keepdims=True)), 1e-12)
    k = k * (1 + (a - 1) * k_a)
    rh, kh, vh, ah = heads(r), heads(k), heads(v), heads(a)
    decay = jnp.exp(-jnp.exp(heads(w)))
    y = _wkv7_scan(rh, decay, kh, vh, -kk, kk * ah)
    mean = jnp.mean(y, axis=-1, keepdims=True)
    var = jnp.mean(jnp.square(y - mean), axis=-1, keepdims=True)
    y = (y - mean) * lax.rsqrt(var + GN_EPS)
    y = y * ln_w.reshape(N_HEADS, HEAD_SIZE) + ln_b.reshape(N_HEADS, HEAD_SIZE)
    bonus = jnp.sum(rh * kh * r_k, axis=-1, keepdims=True) * vh
    out = ((y + bonus).reshape(bsz, seq, d).astype(h.dtype) * g) @ w_o
    return out, v_first

def first_inputs(seed: int = 0) -> dict:
    key = jax.random.key(seed)
    ks = iter(jax.random.split(key, 40))
    D = D_MODEL
    nrm = lambda shape, s: jax.random.normal(next(ks), shape, jnp.float32) * s
    uni = lambda shape, lo, hi: jax.random.uniform(next(ks), shape, jnp.float32, lo, hi)
    NC, NR, NV = N_CONV_LAYERS, N_RWKV_LAYERS, N_VRES
    return {
        "x": nrm((BATCH, SEQ, D), 1.0),
        "c": nrm((BATCH, D), 1.0),
        "norm_g": 1.0 + nrm((DEPTH, 2, D), 0.05),
        "final_g": 1.0 + nrm((D,), 0.05),
        "ada_w": nrm((DEPTH, D, N_MOD * D), 0.5 * D ** -0.5),
        "ada_b": nrm((DEPTH, N_MOD * D), 0.02),
        "conv_w_in": nrm((NC, D, 3 * D), D ** -0.5),
        "conv_w": nrm((NC, CONV_WIDTH, D), CONV_WIDTH ** -0.5),
        "conv_w_out": nrm((NC, D, D), D ** -0.5),
        "rw_mu": uni((NR, 6, D), 0.0, 1.0),
        "rw_w_rkv": nrm((NR, 3, D, D), D ** -0.5),
        "rw_w_o": nrm((NR, D, D), D ** -0.5),
        "rw_w0": uni((NR, D), -6.5, -1.5),
        "rw_w1": nrm((NR, D, D_DECAY_LORA), D ** -0.5),
        "rw_w2": nrm((NR, D_DECAY_LORA, D), 0.1 * D_DECAY_LORA ** -0.5),
        "rw_a0": nrm((NR, D), 0.1),
        "rw_a1": nrm((NR, D, D_AAA_LORA), D ** -0.5),
        "rw_a2": nrm((NR, D_AAA_LORA, D), 0.1 * D_AAA_LORA ** -0.5),
        "rw_g1": nrm((NR, D, D_GATE_LORA), D ** -0.5),
        "rw_g2": nrm((NR, D_GATE_LORA, D), D_GATE_LORA ** -0.5),
        "rw_k_k": 0.85 + nrm((NR, D), 0.05),
        "rw_k_a": 1.0 + nrm((NR, D), 0.05),
        "rw_r_k": nrm((NR, N_HEADS, HEAD_SIZE), 0.1),
        "rw_ln_w": 1.0 + nrm((NR, D), 0.05),
        "rw_ln_b": nrm((NR, D), 0.02),
        "rw_v0": 1.0 + nrm((NV, D), 0.1),
        "rw_v1": nrm((NV, D, D_MV_LORA), D ** -0.5),
        "rw_v2": nrm((NV, D_MV_LORA, D), 0.1 * D_MV_LORA ** -0.5),
        "mlp_w1": nrm((DEPTH, D, D_FF), D ** -0.5),
        "mlp_w2": nrm((DEPTH, D_FF, D), D_FF ** -0.5),
    }

def first_block(x, c, norm_g, final_g, ada_w, ada_b, conv_w_in, conv_w, conv_w_out,
              rw_mu, rw_w_rkv, rw_w_o, rw_w0, rw_w1, rw_w2, rw_a0, rw_a1, rw_a2,
              rw_g1, rw_g2, rw_k_k, rw_k_a, rw_r_k, rw_ln_w, rw_ln_b,
              rw_v0, rw_v1, rw_v2, mlp_w1, mlp_w2):
    c_act = jax.nn.silu(c)
    v_first = None
    for i in range(DEPTH):
        mod = c_act @ ada_w[i] + ada_b[i]
        sh1, sc1, gt1, sh2, sc2, gt2 = jnp.split(mod, N_MOD, axis=-1)
        h = _modulate(_rmsnorm(x, norm_g[i, 0]), sh1, sc1)
        j = i // N_MIXERS
        if i % N_MIXERS == 0:
            y = _short_conv_mixer(h, conv_w_in[j], conv_w[j], conv_w_out[j])
        else:
            vres = None if v_first is None else (rw_v0[j - 1], rw_v1[j - 1], rw_v2[j - 1])
            y, v_first = _rwkv7_mixer(
                h, v_first, vres, rw_mu[j], rw_w_rkv[j], rw_w_o[j], rw_w0[j], rw_w1[j],
                rw_w2[j], rw_a0[j], rw_a1[j], rw_a2[j], rw_g1[j], rw_g2[j], rw_k_k[j],
                rw_k_a[j], rw_r_k[j], rw_ln_w[j], rw_ln_b[j])
        x = x + gt1[:, None, :] * y
        h = _modulate(_rmsnorm(x, norm_g[i, 1]), sh2, sc2)
        x = x + gt2[:, None, :] * (jnp.square(jax.nn.relu(h @ mlp_w1[i])) @ mlp_w2[i])
    return _rmsnorm(x, final_g)


N_A_LAYERS = DEPTH // 2
N_B_LAYERS = DEPTH - N_A_LAYERS

GDN_HEADS = 8
GDN_DK = 128
GDN_DV = 128
GDN_KDIM = GDN_HEADS * GDN_DK
GDN_VDIM = GDN_HEADS * GDN_DV
QKV_DIM = 2 * GDN_KDIM + GDN_VDIM
GDN_PROJ_DIM = QKV_DIM + GDN_VDIM + 2 * GDN_HEADS
CONV_WIDTH_2 = 4

SB_HEADS = 8
SB_DH = D_MODEL // SB_HEADS
SB_DIM = SB_HEADS * SB_DH
Q_BLOCK = 128

D_FF_2 = -(-8 * D_MODEL // (3 * 256)) * 256

EPS = 1e-6


def rms_norm(x, gain):
    xf = x.astype(jnp.float32)
    y = xf * lax.rsqrt(jnp.mean(xf * xf, axis=-1, keepdims=True) + EPS)
    return (y * gain.astype(jnp.float32)).astype(x.dtype)

def l2_norm(x):
    xf = x.astype(jnp.float32)
    return xf * lax.rsqrt(jnp.sum(xf * xf, axis=-1, keepdims=True) + EPS)

def causal_depthwise_conv(x, w):
    c = x.shape[-1]
    return lax.conv_general_dilated(
        x, w[:, None, :].astype(x.dtype), window_strides=(1,),
        padding=[(CONV_WIDTH_2 - 1, 0)], dimension_numbers=('NWC', 'WIO', 'NWC'),
        feature_group_count=c)

def swiglu(x, w_gu, w_down):
    g, u = jnp.split(x @ w_gu, 2, axis=-1)
    return (jax.nn.silu(g) * u) @ w_down

def gated_delta_rule(q, k, v, beta, g):
    b_, h_, s_, dk = q.shape
    dv = v.shape[-1]
    n = s_ // CHUNK
    q = (q * dk ** -0.5).reshape(b_, h_, n, CHUNK, dk)
    k = k.reshape(b_, h_, n, CHUNK, dk)
    v = v.reshape(b_, h_, n, CHUNK, dv)
    beta = beta.reshape(b_, h_, n, CHUNK)
    g_cum = jnp.cumsum(g.reshape(b_, h_, n, CHUNK), axis=-1)

    idx = jnp.arange(CHUNK)
    incl = idx[:, None] >= idx[None, :]
    strict = idx[:, None] > idx[None, :]
    decay = jnp.exp(jnp.where(incl, g_cum[..., :, None] - g_cum[..., None, :], -jnp.inf))

    k_beta = k * beta[..., None]
    a_low = jnp.where(strict, jnp.einsum('bhncd,bhnsd->bhncs', k_beta, k) * decay, 0.0)
    eye = jnp.eye(CHUNK, dtype=q.dtype)
    rhs = jnp.concatenate([v * beta[..., None], k_beta * jnp.exp(g_cum)[..., None]], axis=-1)
    sol = lax.linalg.triangular_solve(eye + a_low, rhs, left_side=True, lower=True,
                                      unit_diagonal=True)
    u, w = sol[..., :dv], sol[..., dv:]

    attn_intra = jnp.einsum('bhncd,bhnsd->bhncs', q, k) * decay
    g_last = g_cum[..., -1]
    k_decay = k * jnp.exp(g_last[..., None] - g_cum)[..., None]
    q_decay = q * jnp.exp(g_cum)[..., None]

    def step(state, inp):
        qd, kd, ui, wi, ai, gl = inp
        v_new = ui - jnp.einsum('bhck,bhkv->bhcv', wi, state)
        o = (jnp.einsum('bhck,bhkv->bhcv', qd, state)
             + jnp.einsum('bhcs,bhsv->bhcv', ai, v_new))
        state = state * jnp.exp(gl)[..., None, None] + jnp.einsum('bhck,bhcv->bhkv', kd, v_new)
        return state, o

    xs = tuple(jnp.moveaxis(t, 2, 0) for t in (q_decay, k_decay, u, w, attn_intra, g_last))
    state0 = jnp.zeros((b_, h_, dk, dv), q.dtype)
    _, o = lax.scan(step, state0, xs)
    return jnp.moveaxis(o, 0, 2).reshape(b_, h_, s_, dv)

def gdn_mixer(hn, w_in, conv_w, a_log, dt_bias, o_gain, w_out):
    b_, s_, _ = hn.shape
    f32 = jnp.float32
    proj = hn @ w_in
    qkv, z, b_raw, a_raw = jnp.split(
        proj, [QKV_DIM, QKV_DIM + GDN_VDIM, QKV_DIM + GDN_VDIM + GDN_HEADS], axis=-1)
    qkv = jax.nn.silu(causal_depthwise_conv(qkv, conv_w))
    q, k, v = jnp.split(qkv, [GDN_KDIM, 2 * GDN_KDIM], axis=-1)

    def heads(t, d):
        return t.reshape(b_, s_, GDN_HEADS, d).transpose(0, 2, 1, 3)

    q = l2_norm(heads(q, GDN_DK))
    k = l2_norm(heads(k, GDN_DK))
    v = heads(v, GDN_DV).astype(f32)
    beta = jax.nn.sigmoid(b_raw.astype(f32)).transpose(0, 2, 1)
    g = (-jnp.exp(a_log.astype(f32))
         * jax.nn.softplus(a_raw.astype(f32) + dt_bias.astype(f32))).transpose(0, 2, 1)
    o = gated_delta_rule(q, k, v, beta, g).transpose(0, 2, 1, 3)
    zf = z.reshape(b_, s_, GDN_HEADS, GDN_DV).astype(f32)
    o = rms_norm(o, o_gain) * jax.nn.silu(zf)
    return o.reshape(b_, s_, GDN_VDIM).astype(hn.dtype) @ w_out

def shared_kv(h, kv_norm, w_kv, k_gain):
    b_, s_, _ = h.shape
    k, v = jnp.split(rms_norm(h, kv_norm) @ w_kv, 2, axis=-1)
    k = rms_norm(k.reshape(b_, s_, SB_HEADS, SB_DH), k_gain).transpose(0, 2, 1, 3)
    v = v.reshape(b_, s_, SB_HEADS, SB_DH).transpose(0, 2, 1, 3)
    return k, v

def stick_breaking_attention(q, k, v):
    _, _, s_, dh = q.shape
    f32 = jnp.float32
    scale = dh ** -0.5
    outs = []
    for blk in range(s_ // Q_BLOCK):
        t0 = blk * Q_BLOCK
        end = t0 + Q_BLOCK
        qb = q[:, :, t0:end].astype(f32)
        kb = k[:, :, :end].astype(f32)
        vb = v[:, :, :end].astype(f32)
        z = jnp.einsum('bhtd,bhsd->bhts', qb, kb) * scale
        t_idx = t0 + jnp.arange(Q_BLOCK)
        s_idx = jnp.arange(end)
        causal = s_idx[None, :] < t_idx[:, None]
        ls_neg = jax.nn.log_sigmoid(-z)
        log_fail = jnp.where(causal, ls_neg, 0.0)
        log_rest = lax.cumsum(log_fail, axis=3, reverse=True) - log_fail
        log_a = z + ls_neg + log_rest
        att = jnp.where(causal, jnp.exp(log_a), 0.0)
        outs.append(jnp.einsum('bhts,bhsd->bhtd', att, vb))
    return jnp.concatenate(outs, axis=2).astype(q.dtype)

def sb_mixer(hn, k_sh, v_sh, w_q, q_gain, w_out):
    b_, s_, _ = hn.shape
    q = rms_norm((hn @ w_q).reshape(b_, s_, SB_HEADS, SB_DH), q_gain).transpose(0, 2, 1, 3)
    o = stick_breaking_attention(q, k_sh, v_sh)
    return o.transpose(0, 2, 1, 3).reshape(b_, s_, SB_DIM).astype(hn.dtype) @ w_out

def second_inputs(seed: int = 0) -> dict:
    key = jax.random.key(seed)
    ks = jax.random.split(key, 17)
    f32 = jnp.float32

    def dense(k, shape, fan_in, scale=1.0):
        return jax.random.normal(k, shape, f32) * (scale * fan_in ** -0.5)

    def gain(k, shape):
        return 1.0 + 0.02 * jax.random.normal(k, shape, f32)

    out_scale = (2 * DEPTH) ** -0.5
    x = jax.random.normal(ks[0], (BATCH, SEQ, D_MODEL), f32)
    attn_norm = gain(ks[1], (DEPTH, D_MODEL))
    ffn_norm = gain(ks[2], (DEPTH, D_MODEL))
    gdn_w_in = dense(ks[3], (N_A_LAYERS, D_MODEL, GDN_PROJ_DIM), D_MODEL)
    gdn_conv_w = jax.random.normal(ks[4], (N_A_LAYERS, CONV_WIDTH_2, QKV_DIM), f32) * CONV_WIDTH_2 ** -0.5
    gdn_a_log = jnp.log(jax.random.uniform(ks[5], (N_A_LAYERS, GDN_HEADS), f32, 1.0, 16.0))
    dt = jnp.exp(jax.random.uniform(ks[6], (N_A_LAYERS, GDN_HEADS), f32,
                                    math.log(1e-3), math.log(1e-1)))
    gdn_dt_bias = dt + jnp.log(-jnp.expm1(-dt))
    gdn_o_gain = gain(ks[7], (N_A_LAYERS, GDN_DV))
    gdn_w_out = dense(ks[8], (N_A_LAYERS, GDN_VDIM, D_MODEL), GDN_VDIM, out_scale)
    kv_norm = gain(ks[9], (D_MODEL,))
    w_kv = dense(ks[10], (D_MODEL, 2 * SB_DIM), D_MODEL)
    k_gain = gain(ks[11], (SB_DH,))
    sb_w_q = dense(ks[12], (N_B_LAYERS, D_MODEL, SB_DIM), D_MODEL)
    sb_q_gain = gain(ks[13], (N_B_LAYERS, SB_DH))
    sb_w_out = dense(ks[14], (N_B_LAYERS, SB_DIM, D_MODEL), SB_DIM, out_scale)
    ffn_w_gu = dense(ks[15], (DEPTH, D_MODEL, 2 * D_FF_2), D_MODEL)
    ffn_w_down = dense(ks[16], (DEPTH, D_FF_2, D_MODEL), D_FF_2, out_scale)
    return {"x": x, "attn_norm": attn_norm, "ffn_norm": ffn_norm,
            "gdn_w_in": gdn_w_in, "gdn_conv_w": gdn_conv_w, "gdn_a_log": gdn_a_log,
            "gdn_dt_bias": gdn_dt_bias, "gdn_o_gain": gdn_o_gain, "gdn_w_out": gdn_w_out,
            "kv_norm": kv_norm, "w_kv": w_kv, "k_gain": k_gain,
            "sb_w_q": sb_w_q, "sb_q_gain": sb_q_gain, "sb_w_out": sb_w_out,
            "ffn_w_gu": ffn_w_gu, "ffn_w_down": ffn_w_down}

def second_block(x, attn_norm, ffn_norm, gdn_w_in, gdn_conv_w, gdn_a_log, gdn_dt_bias,
              gdn_o_gain, gdn_w_out, kv_norm, w_kv, k_gain, sb_w_q, sb_q_gain, sb_w_out,
              ffn_w_gu, ffn_w_down):
    h = x
    k_sh = None
    v_sh = None
    for layer in range(DEPTH):
        hn = rms_norm(h, attn_norm[layer])
        if layer < N_A_LAYERS:
            i = layer
            h = h + gdn_mixer(hn, gdn_w_in[i], gdn_conv_w[i], gdn_a_log[i], gdn_dt_bias[i],
                              gdn_o_gain[i], gdn_w_out[i])
        else:
            if layer == N_A_LAYERS:
                k_sh, v_sh = shared_kv(h, kv_norm, w_kv, k_gain)
            j = layer - N_A_LAYERS
            h = h + sb_mixer(hn, k_sh, v_sh, sb_w_q[j], sb_q_gain[j], sb_w_out[j])
        h = h + swiglu(rms_norm(h, ffn_norm[layer]), ffn_w_gu[layer], ffn_w_down[layer])
    return h


def setup_inputs(seed=0):
    out = dict(first_inputs(seed))
    for name, value in second_inputs(seed + 1).items():
        if name != "x":
            out[name + "_2"] = value
    return out


def reference(
    x, c, norm_g, final_g, ada_w, ada_b, conv_w_in, conv_w, conv_w_out, rw_mu, rw_w_rkv, rw_w_o,
    rw_w0, rw_w1, rw_w2, rw_a0, rw_a1, rw_a2, rw_g1, rw_g2, rw_k_k, rw_k_a, rw_r_k, rw_ln_w,
    rw_ln_b, rw_v0, rw_v1, rw_v2, mlp_w1, mlp_w2, attn_norm_2, ffn_norm_2, gdn_w_in_2,
    gdn_conv_w_2, gdn_a_log_2, gdn_dt_bias_2, gdn_o_gain_2, gdn_w_out_2, kv_norm_2, w_kv_2,
    k_gain_2, sb_w_q_2, sb_q_gain_2, sb_w_out_2, ffn_w_gu_2, ffn_w_down_2,
):
    x = first_block(
        x, c, norm_g, final_g, ada_w, ada_b, conv_w_in, conv_w, conv_w_out, rw_mu, rw_w_rkv,
        rw_w_o, rw_w0, rw_w1, rw_w2, rw_a0, rw_a1, rw_a2, rw_g1, rw_g2, rw_k_k, rw_k_a, rw_r_k,
        rw_ln_w, rw_ln_b, rw_v0, rw_v1, rw_v2, mlp_w1, mlp_w2,
    )
    return second_block(
        x, attn_norm_2, ffn_norm_2, gdn_w_in_2, gdn_conv_w_2, gdn_a_log_2, gdn_dt_bias_2,
        gdn_o_gain_2, gdn_w_out_2, kv_norm_2, w_kv_2, k_gain_2, sb_w_q_2, sb_q_gain_2,
        sb_w_out_2, ffn_w_gu_2, ffn_w_down_2,
    )


_drawn_inputs = setup_inputs


def setup_inputs(seed=0):
    import zlib

    import numpy as np

    out = dict(_drawn_inputs(seed))
    spreads = {}
    factors = {'rw_w1': 8.0,
     'rw_w2': 8.0,
     'rw_a0': 7.363,
     'rw_a1': 7.137,
     'rw_a2': 7.176,
     'rw_k_k': 2.97,
     'rw_ln_w': 7.011,
     'rw_ln_b': 8.0,
     'attn_norm_2': 5.245,
     'ffn_norm_2': 5.213,
     'gdn_o_gain_2': 8.0,
     'kv_norm_2': 24.507,
     'k_gain_2': 24.186,
     'sb_q_gain_2': 23.656}
    for name, (base, spread) in spreads.items():
        noise = np.random.default_rng([zlib.crc32(name.encode()), seed]).standard_normal(out[name].shape)
        drawn = base * np.exp(spread * noise) if base else spread * noise
        out[name] = __import__('jax').numpy.asarray(drawn.astype(out[name].dtype))
    for name, factor in factors.items():
        out[name] = (out[name] * factor).astype(out[name].dtype)
    return out
```

```python
from contextlib import ExitStack

import numpy as np
import concourse.bass as bass
from concourse import mybir
from concourse.alu_op_type import AluOpType as ALU

F32 = mybir.dt.float32
F32R = mybir.dt.float32r
ACT = mybir.ActivationFunctionType

P = 128
T = 512
KT = 8
D = 1024

COLS = {}


def _cols():
    at = 0
    for name, n in [("c", 8), ("norm_g", 32), ("final_g", 8), ("ada_b", 96), ("conv_w", 24), ("mu", 48),
                    ("w0", 8), ("a0", 8), ("k_k", 8), ("k_a", 8), ("r_k", 8), ("ln_w", 8), ("ln_b", 8),
                    ("attn_norm", 16), ("ffn_norm", 16), ("kv_norm", 8), ("gconv", 96),
                    ("o_gain", 1), ("k_gain", 1), ("q_gain", 1), ("a_log", 1), ("dt_bias", 1)]:
        COLS[name] = (at, n)
        at += n
    return at


NCOL = _cols()

TAB = {}
NMAIN = 7 * P + 64


def tables():
    i = np.arange(P)[:, None]
    j = np.arange(P)[None, :]
    parts = []

    def put(name, a):
        TAB[name] = (sum(x.shape[1] for x in parts), a.shape[1])
        parts.append(np.ascontiguousarray(np.broadcast_to(a, (P, a.shape[1])), dtype=np.float32))

    put("ones", np.ones((P, P)))
    put("ident", (i == j))
    put("bones", (i // 64 == j // 64))
    put("tri", (i >= j))
    put("sup", (i < j))
    put("supi", (i <= j))
    put("rwm", np.concatenate([(i % 64 < j[:, :64]), (i % 64 <= j[:, :64])], axis=1))
    put("idk", np.concatenate([np.eye(64), np.eye(64)], axis=0))
    for n in range(7):
        m = 1 << n
        put(f"low{n}", (i // (2 * m) == j // (2 * m)) & (i % (2 * m) >= m) & (j % (2 * m) < m))
    put("upp0", (i // 2 == j // 2) & (i < j))
    return np.concatenate(parts, axis=1)


NTAB = tables().shape[1]

STREAM = {
    "cin": (12, 8, 256), "cout": (4, 8, 256), "m1": (32, 8, 256), "m2": (32, 16, 128),
    "lwa": (1, 8, 128), "lg": (1, 8, 160), "rkv": (12, 8, 256), "wo": (4, 8, 256),
    "gab": (1, 8, 128), "gin": (16, 8, 256), "gout": (4, 8, 256), "kv": (8, 8, 256), "sq": (4, 8, 256),
    "so": (4, 8, 256), "gu": (44, 8, 256), "dn": (32, 11, 128),
}


def order():
    out = []

    def add(name, a, b):
        out.extend((name, i) for i in range(a, b))

    def mlp(layer):
        for g in range(2):
            add("m1", 16 * layer + 8 * g, 16 * layer + 8 * g + 8)
            add("m2", 16 * layer + 8 * g, 16 * layer + 8 * g + 8)

    def ffn(layer):
        for g in range(2):
            add("gu", 22 * layer + 11 * g, 22 * layer + 11 * g + 11)
            add("dn", 16 * layer + 8 * g, 16 * layer + 8 * g + 8)

    add("cin", 0, 12)
    add("cout", 0, 4)
    mlp(0)
    add("lwa", 0, 1)
    add("lg", 0, 1)
    add("rkv", 0, 12)
    add("wo", 0, 4)
    mlp(1)
    add("gab", 0, 1)
    add("gin", 0, 16)
    add("gout", 0, 4)
    ffn(0)
    add("kv", 0, 8)
    add("sq", 0, 4)
    add("so", 0, 4)
    ffn(1)
    return out


class Op:

    def __init__(self, eng, fn, waits):
        self.eng, self.fn, self.waits = eng, fn, waits
        self.used, self.val = False, 0


class Dma:

    def __init__(self, sem, val):
        self.sem, self.val = sem, val


class Queues:

    def __init__(self, nc, ctx):
        self.nc = nc
        self.q = {e: [] for e in ("pe", "act", "dve", "pool", "sp")}
        self.sem = {e: ctx.enter_context(nc.semaphore("s_" + e)) for e in ("pe", "act", "dve", "pool")}
        self.ctx = ctx
        self.stores = []

    def add(self, eng, fn, waits):
        flat = []

        def walk(w):
            if w is None:
                return
            if isinstance(w, (list, tuple)):
                for x in w:
                    walk(x)
            else:
                flat.append(w)
                if isinstance(w, Op):
                    w.used = True

        walk(waits)
        op = Op(eng, fn, flat)
        self.q[eng].append(op)
        return op

    def pe(self, fn, *w):
        return self.add("pe", fn, w)

    def act(self, fn, *w):
        return self.add("act", fn, w)

    def dve(self, fn, *w):
        return self.add("dve", fn, w)

    def pool(self, fn, *w):
        return self.add("pool", fn, w)

    def dma(self, eng, dst, src, sem, count, *w):
        self.add(eng, lambda e: e.dma_start(dst, src).then_inc(sem, 16), w)
        return Dma(sem, 16 * (count + 1))

    def last(self, *engs):
        return [self.q[e][-1] for e in engs if self.q[e]]

    def emit(self, eng, e):
        n, seen = 0, {}
        for op in self.q[eng]:
            need = {}
            for w in op.waits:
                sem, val = (self.sem[w.eng], w.val) if isinstance(w, Op) else (w.sem, w.val)
                key = sem.name
                if val > seen.get(key, 0) and val > need.get(key, (None, 0))[1]:
                    need[key] = (sem, val)
            for key, (sem, val) in need.items():
                e.wait_ge(sem, val)
                seen[key] = val
            ins = op.fn(e)
            if op.used:
                ins.then_inc(self.sem[eng], 1)

    def number(self):
        for ops in self.q.values():
            n = 0
            for op in ops:
                if op.used:
                    n += 1
                    op.val = n


class Banks:

    def __init__(self, tiles):
        self.tiles, self.free, self.n = tiles, [None] * len(tiles), 0

    def get(self):
        i = self.n % len(self.tiles)
        self.n += 1
        return i, self.tiles[i], self.free[i]

    def done(self, i, *ops):
        self.free[i] = list(ops)


def build(nc, x, cols, tab, ada, w, lo2, out, stop=None, dbg=None):
    ctx = ExitStack()
    with ctx:
        Q = Queues(nc, ctx)
        at = [16512]

        def place(name, shape, dt, off=None):
            size = 4 * int(np.prod(shape[1:]))
            if off is None:
                off = at[0]
                at[0] += (size + 31) // 32 * 32
            return nc.alloc_sbuf_tensor_at(name, shape, dt, offset=off)

        X = place("X", [P, KT, T], F32)
        HH = place("HH", [P, KT, T], F32R)
        HL = place("HL", [P, KT, T], F32R)
        w_at = at[0]
        ST = place("ST", [P, 3, 2048], F32)
        WH = place("WH", [P, 3, 2048], F32R)
        WL = place("WL", [P, 3, 2048], F32R)
        ar_at = at[0]
        at[0] += 67648
        GH = place("GH", [P, 16, T], F32R, ar_at)
        GL = place("GL", [P, 16, T], F32R, ar_at + 32768)
        CC = place("CC", [P, NCOL], F32)
        TB = place("TB", [P, NMAIN], F32)
        MOD = place("MOD", [P, 96], F32)
        ADR = place("ADR", [P, 2, 512], F32)
        ADA = place("ADA", [P, 512], F32)
        RST = place("RST", [P, T], F32)
        ACC = place("ACC", [P, T], F32)
        TMP = place("TMP", [P, 2, T], F32)
        SM = place("SM", [P, 64], F32)
        assert at[0] <= 229368, at[0]

        def col(name, i=0):
            a, n = COLS[name]
            assert i < n
            return CC[:, a + i:a + i + 1]

        def tb(name, rows=slice(0, P)):
            a, n = TAB[name]
            return TB[rows, a:a + n]

        PS = [ctx.enter_context(nc.psum_tensor(f"ps{i}", [P, 512], F32)) for i in range(8)]
        big = Banks(PS[0:4])
        sml = Banks(PS[4:8])

        sem = {}

        def semaphore(name):
            sem[name] = ctx.enter_context(nc.semaphore(name))
            return sem[name]

        s_x, s_cols, s_tab = semaphore("s_x"), semaphore("s_cols"), semaphore("s_tab")
        s_st = [semaphore(f"s_st{i}") for i in range(3)]
        s_ad = [semaphore(f"s_ad{i}") for i in range(2)]
        s_lo = semaphore("s_lo")
        s_out = semaphore("s_out")

        sched = order()

        class Weights:
            def __init__(self):
                self.loads, self.splits = 0, 0
                self.landed, self.split, self.used = {}, {}, {}
                self.limit, self.fence = len(sched), []
                self.turns = [0, 0, 0]

            def shape(self, j):
                name, i = sched[j]
                n, kt, c = STREAM[name]
                return w[name][i], kt, c

            def load(self):
                j = self.loads
                if j >= min(len(sched), self.limit):
                    return
                self.loads += 1
                s = j % 3
                src, kt, c = self.shape(j)
                self.landed[j] = Q.dma("sp", ST[:, s, 0:kt * c], src, s_st[s], self.turns[s],
                                       self.split.get(j - 3), self.fence)
                self.turns[s] += 1

            def cut(self, upto):
                while self.splits <= min(upto, len(sched) - 1, self.limit - 1):
                    j = self.splits
                    while self.loads <= j:
                        self.load()
                    self.splits += 1
                    s = j % 3
                    _, kt, c = self.shape(j)
                    n = kt * c
                    hi = Q.act(lambda e, s=s, n=n: e.activation(WH[:, s, 0:n], ST[:, s, 0:n], ACT.Copy),
                               self.landed[j], self.used.get(j - 3), self.fence)
                    lo = Q.dve(lambda e, s=s, n=n: e.tensor_tensor(
                        WL[:, s, 0:n], ST[:, s, 0:n], WH[:, s, 0:n].bitcast(F32), ALU.subtract), hi)
                    self.split[j] = [hi, lo]
                    while self.loads < j + 4 and self.loads < min(len(sched), self.limit):
                        self.load()

            def take(self, j):
                self.cut(j + 2)
                s = j % 3
                _, kt, c = self.shape(j)

                def view(W):
                    return W[:, s, 0:kt * c].rearrange("p (k c) -> p k c", k=kt)
                return view(WH), view(WL), self.split[j]

        W = Weights()
        turn = [0]

        def next_chunk():
            turn[0] += 1
            return turn[0] - 1

        d_cols = Q.dma("sp", CC[:, :], cols, s_cols, 0)
        d_x = Q.dma("sp", X[:, :, :], x, s_x, 0)
        d_tab = Q.dma("act", TB[:, :], tab[:, 0:NMAIN], s_tab, 0)

        o_cs = Q.act(lambda e: e.activation(SM[:, 0:8], CC[:, 0:8], ACT.Silu), d_cols)

        class Ada:

            def __init__(self):
                self.n = self.loads = 0
                self.read, self.landed = {}, {}
                self.acc, self.used = None, None
                self.cols = {}

            def load(self):
                if self.loads >= 192:
                    return
                n = self.loads
                self.loads += 1
                s = n % 2
                self.landed[n] = Q.dma("pool", ADR[:, s, :], ada[n], s_ad[s], n // 2, self.read.get(n - 2))

            def step(self):
                if self.n >= 192:
                    return
                n = self.n
                self.n += 1
                while self.loads <= n:
                    self.load()
                s, k, blk = n % 2, n % 8, n // 8
                cc = SM[:, k:k + 1]
                if k == 0:
                    o = Q.dve(lambda e: e.tensor_scalar(ADA[:, :], ADR[:, s, :], cc, None, ALU.mult),
                              self.landed[n], o_cs, self.used)
                else:
                    o = Q.dve(lambda e: e.scalar_tensor_tensor(out=ADA[:, :], in0=ADR[:, s, :], scalar=cc,
                                                               in1=ADA[:, :], op0=ALU.mult, op1=ALU.add),
                              self.landed[n], self.acc)
                self.acc = self.read[n] = o
                self.load()
                if k == 7:
                    i, ps, free = sml.get()
                    for j in range(4):
                        m = Q.pe(lambda e, j=j, ps=ps: e.matmul(ps[:, j:j + 1], ADA[:, 128 * j:128 * j + 128],
                                                         tb("ones")[:, 0:1], start=True, stop=True),
                                 o, free, d_tab)
                    self.used = m
                    a = COLS["ada_b"][0] + 4 * blk
                    o = Q.dve(lambda e, ps=ps: e.tensor_tensor(MOD[:, 4 * blk:4 * blk + 4], ps[:, 0:4],
                                                        CC[:, a:a + 4], ALU.add), m)
                    sml.done(i, o)
                    for j in range(4):
                        self.cols[4 * blk + j] = o

            def need(self, layer, which):
                last = 48 * layer + 8 * which + 7
                while last not in self.cols:
                    self.step()
                return self.cols[last]

        A = Ada()

        def modcol(layer, which, k):
            a = 48 * layer + 8 * which + k
            return MOD[:, a:a + 1]

        tmp_free = [None, None]
        tmp_n = [0]

        def tmp():
            i = tmp_n[0] % 2
            tmp_n[0] += 1
            return i, TMP[:, i, :], tmp_free[i]

        rms_state = {"acc": None, "acc_free": None, "rst_free": None}

        def square_add(k, ready):
            i, t, free = tmp()
            if k == 0:
                o = Q.act(lambda e: e.activation(ACC[:, :], X[:, k, :], ACT.Square), ready,
                          rms_state["acc_free"])
                rms_state["acc"] = o
                return
            o = Q.act(lambda e: e.activation(t, X[:, k, :], ACT.Square), ready, free)
            o = Q.pool(lambda e: e.tensor_tensor(ACC[:, :], ACC[:, :], t, ALU.add), o, rms_state["acc"])
            tmp_free[i] = o
            rms_state["acc"] = o

        def rms():
            i, ps, free = sml.get()
            m = Q.pe(lambda e, ps=ps: e.matmul(ps[:, :], tb("ones"), ACC[:, :], start=True, stop=True),
                     rms_state["acc"], free, d_tab)
            rms_state["acc_free"] = m
            o = Q.dve(lambda e, ps=ps: e.tensor_scalar(RST[:, :], ps[:, :], 1.0 / D, 1e-6, ALU.mult, ALU.add), m,
                      rms_state["rst_free"])
            sml.done(i, o)
            o = Q.act(lambda e: e.activation(RST[:, :], RST[:, :], ACT.Sqrt), o)
            return Q.dve(lambda e: e.reciprocal(RST[:, :], RST[:, :]), o)

        def split_into(H, L, src, ready, free, bias=0.0):
            h = Q.act(lambda e: e.activation(H, src, ACT.Identity, bias=bias), ready, free)
            if isinstance(bias, float):
                lo = Q.dve(lambda e: e.tensor_tensor(L, src, H.bitcast(F32), ALU.subtract), h)
            else:
                lo = Q.dve(lambda e: e.scalar_tensor_tensor(out=L, in0=src, scalar=bias, in1=H.bitcast(F32),
                                                            op0=ALU.add, op1=ALU.subtract), h)
            return [h, lo]

        gain = {}

        def mod_gain(name, gname, g0, layer, which):
            o = A.need(layer, which)
            s = 8 + 8 * (len(gain) % 4)
            a = 48 * layer + 8 * which
            g = COLS[gname][0] + g0
            o = Q.dve(lambda e: e.scalar_tensor_tensor(out=SM[:, s:s + 8], in0=MOD[:, a:a + 8], scalar=1.0,
                                                       in1=CC[:, g:g + 8], op0=ALU.add, op1=ALU.mult),
                      o, d_cols)
            gain[name] = s
            return lambda k: SM[:, s + k:s + k + 1], o

        h_free = [None]

        def norm_split(gcol, gready, bcol, rstd):
            ready = []
            for k in range(KT):
                i, t, free = tmp()
                o = Q.dve(lambda e, k=k, t=t: e.scalar_tensor_tensor(
                    out=t, in0=X[:, k, :], scalar=gcol(k), in1=RST[:, :], op0=ALU.mult, op1=ALU.mult),
                    rstd, gready, free)
                b = bcol(k) if bcol else 0.0
                r = split_into(HH[:, k, :], HL[:, k, :], t, o, h_free[0], b)
                tmp_free[i] = r
                ready.append(r)
            rms_state["rst_free"] = o
            return ready

        def dense(nchunk, H, L, ready, consume, first=None, cols=None, side=None):
            m = 0
            for n in range(nchunk):
                j = next_chunk()
                wh, wl, cut = W.take(j)
                _, kt, c = W.shape(j)
                for c0 in (cols or range(0, c, P)):
                    i, ps, free = big.get()
                    for k in range(kt):
                        for part, (a, b) in enumerate(((wh, H), (wh, L), (wl, H))):
                            o = Q.pe(lambda e, ps=ps, a=a, b=b, k=k, c0=c0, part=part, kt=kt: e.matmul(
                                ps[:, :], a[:, k, c0:c0 + P], b[:, k, :], start=(k == 0 and part == 0),
                                stop=(k == kt - 1 and part == 2)), free, cut, ready[k], first)
                    big.done(i, *consume(m, ps, o))
                    m += 1
                W.used[j] = o
                if side:
                    side(n)
            return o

        def residual(gcol, gready, squares):
            def consume(m, ps, o):
                if gcol is None:
                    r = Q.dve(lambda e, ps=ps: e.tensor_tensor(X[:, m, :], X[:, m, :], ps[:, :], ALU.add), o)
                else:
                    r = Q.dve(lambda e, ps=ps: e.scalar_tensor_tensor(out=X[:, m, :], in0=ps[:, :], scalar=gcol(m),
                                                               in1=X[:, m, :], op0=ALU.mult, op1=ALU.add),
                              o, gready)
                x_ready[m] = r
                if squares:
                    square_add(m, r)
                return [r]
            return consume

        x_ready = [d_x] * KT

        def finish():
            o = x_ready
            Q.dma("sp", out, X[:, :, :], s_out, 0, o)

        g_free = [None] * 16

        def mlp(layer):
            gc, gr = mod_gain(f"mlp{layer}", "norm_g", 16 * layer + 8, layer, 4)
            br = A.need(layer, 3)
            ready = norm_split(gc, [gr, br], lambda k: modcol(layer, 3, k), rms())
            gt = A.need(layer, 5)
            for g in range(2):
                gready = [None] * 16

                def hidden(m, ps, o):
                    i, t, free = tmp()
                    r = Q.act(lambda e, ps=ps: e.activation(t, ps[:, :], ACT.Relu), o, free)
                    s = Q.act(lambda e: e.activation(t, t, ACT.Square), r)
                    h = split_into(GH[:, m, :], GL[:, m, :], t, s, g_free[m])
                    tmp_free[i] = h
                    gready[m] = h
                    return [r]

                h_free[0] = dense(8, HH, HL, ready, hidden, side=lambda n: [A.step() for _ in range(4)])
                last = dense(8, GH, GL, gready, residual(lambda m: modcol(layer, 5, m), gt, g == 1),
                             side=lambda n: [A.step() for _ in range(3)])
                for m in range(16):
                    g_free[m] = last

        def conv_mixer():
            for k in range(KT):
                square_add(k, d_x)
            rstd = rms()
            gc, gr = mod_gain("conv", "norm_g", 0, 0, 1)
            br = A.need(0, 0)
            ready = norm_split(gc, [gr, br], lambda k: modcol(0, 0, k), rstd)
            U = place("U", [P, 2, T + 2], F32, ar_at + 32768 + 16384)
            CV = place("CV", [P, 2, T], F32, ar_at + 32768 + 16384 + 8192)
            z = Q.pool(lambda e: e.memset(U[:, :, 0:2], 0.0))
            u_free, cv, yready = [None, None], [None, None], [None] * KT
            cs = {}

            def consume(m, ps, o):
                grp, r = m // 6, m % 6
                if r in (0, 2):
                    f = r // 2
                    i, t, free = tmp()
                    c = Q.act(lambda e, ps=ps: e.activation(t, ps[:, :], ACT.Copy), o, free)
                    cs[f] = (i, t, c)
                    return [c]
                if r in (1, 3):
                    f = r // 2
                    k = 2 * grp + f
                    i, t, c = cs[f]
                    u = Q.dve(lambda e, ps=ps: e.tensor_tensor(U[:, f, 2:T + 2], ps[:, :], t, ALU.mult), o, c, z,
                              u_free[f])
                    tmp_free[i] = u
                    a = Q.dve(lambda e: e.tensor_scalar(CV[:, f, :], U[:, f, 0:T], col("conv_w", k), None,
                                                        ALU.mult), u, cv[f])
                    for j in (1, 2):
                        a = Q.dve(lambda e, j=j: e.scalar_tensor_tensor(
                            out=CV[:, f, :], in0=U[:, f, j:j + T], scalar=col("conv_w", 8 * j + k),
                            in1=CV[:, f, :], op0=ALU.mult, op1=ALU.add), a)
                    u_free[f] = a
                    cv[f] = a
                    return [u]
                f = r - 4
                k = 2 * grp + f
                y = Q.dve(lambda e, ps=ps: e.tensor_tensor(CV[:, f, :], CV[:, f, :], ps[:, :], ALU.mult), o, cv[f])
                h = split_into(GH[:, k, :], GL[:, k, :], CV[:, f, :], y, None)
                cv[f] = h
                yready[k] = h
                return [y]

            h_free[0] = dense(12, HH, HL, ready, consume, side=lambda n: [A.step() for _ in range(4)])
            gt = A.need(0, 2)
            last = dense(4, GH, GL, yready, residual(lambda m: modcol(0, 2, m), gt, True))
            for m in range(16):
                g_free[m] = [last] + Q.last("dve", "act")

        def inverse(lt, tt, t, u, tb2, levels, banks, ready):
            n_mat = lt.shape[1]
            halves = [range(a, min(a + 4, n_mat)) for a in range(0, n_mat, 4)]
            tt_o, t_o, u_free = {}, {}, {}
            for h, r in enumerate(halves):
                i, ps, free = banks.get()
                for n in r:
                    c = P * (n - r[0])
                    o = Q.pe(lambda e, n=n, c=c, ps=ps: e.transpose(ps[:, c:c + P], tt[:, n, :], tb("ident")),
                             ready, free)
                w_ = P * len(r)
                o = Q.act(lambda e, r=r, ps=ps, w_=w_: e.activation(
                    t[:, r[0]:r[-1] + 1, :], ps[:, 0:w_].rearrange("p (n c) -> p n c", c=P), ACT.Copy), o)
                banks.done(i, o)
                t_o[h], tt_o[h] = [o], [ready]
            yield
            for lev in range(1, levels):
                mask = tb2(f"low{lev}")
                for h, r in enumerate(halves):
                    a, b = r[0], r[-1] + 1
                    k = len(r)
                    i, ps, free = banks.get()
                    for n in r:
                        c = P * (n - a)
                        o = Q.pe(lambda e, n=n, c=c, ps=ps: e.matmul(ps[:, c:c + P], lt[:, n, :], t[:, n, :],
                                                                     start=True, stop=True),
                                 t_o[h], free)
                    mb = mask[:, None, :].broadcast_to((P, k, P))
                    uo = Q.dve(lambda e, a=a, b=b, ps=ps, mb=mb, k=k: e.tensor_tensor(
                        u[:, a:b, :], ps[:, 0:P * k].rearrange("p (n c) -> p n c", c=P), mb, ALU.mult),
                        o, u_free.get(h))
                    banks.done(i, uo)
                    u_free[h] = uo
                yield
                for h, r in enumerate(halves):
                    a, b = r[0], r[-1] + 1
                    k = len(r)
                    more = lev < levels - 1
                    if more:
                        i, ps, free = banks.get()
                        for n in r:
                            c = P * (n - a)
                            o1 = Q.pe(lambda e, n=n, c=c, ps=ps: e.matmul(
                                ps[:, c:c + P], tt[:, n, :], u[:, n, :], start=True, stop=True),
                                u_free[h], tt_o[h], free)
                        o = Q.dve(lambda e, a=a, b=b, ps=ps, k=k: e.tensor_tensor(
                            t[:, a:b, :], t[:, a:b, :], ps[:, 0:P * k].rearrange("p (n c) -> p n c", c=P),
                            ALU.add), o1)
                        banks.done(i, o)
                        t_o[h] = [o]
                    i, ps, free = banks.get()
                    for n in r:
                        c = P * (n - a)
                        o2 = Q.pe(lambda e, n=n, c=c, ps=ps: e.matmul(
                            ps[:, c:c + P], u[:, n, :], tt[:, n, :], start=True, stop=True),
                            u_free[h], tt_o[h], free)
                    o = Q.dve(lambda e, a=a, b=b, ps=ps, k=k: e.tensor_tensor(
                        tt[:, a:b, :], tt[:, a:b, :], ps[:, 0:P * k].rearrange("p (n c) -> p n c", c=P),
                        ALU.add), o2)
                    banks.done(i, o)
                    tt_o[h] = [o]
                    u_free[h] = [o2]
                yield
            yield [o for v in tt_o.values() for o in v]

        def interleave(*gens):
            gens = list(gens)
            while gens:
                gens = [g for g in gens if next(g, gens) is not gens]

        def rwkv_mixer():
            NE = float(np.exp(-0.5))
            A.need(1, 5)
            rstd = rms()
            gc, gr = mod_gain("rwkv", "norm_g", 16, 1, 1)
            HT = place("HT", [P, KT, T + 1], F32, ar_at)
            base = ar_at + 16448
            RR = place("RR", [P, KT, T], F32, base)
            KK = place("KK", [P, KT, T], F32, base + 16384)
            VV = place("VV", [P, KT, T], F32, base + 32768)
            XX = place("XX", [P, 512], F32, base + 49152)
            fence = Q.last("pe", "act", "dve", "pool")
            z = Q.pool(lambda e: e.memset(HT[:, :, 0:1], 0.0), fence)
            ht = []
            for k in range(KT):
                i, t, free = tmp()
                o = Q.dve(lambda e, k=k, t=t: e.scalar_tensor_tensor(
                    out=t, in0=X[:, k, :], scalar=gc(k), in1=RST[:, :], op0=ALU.mult, op1=ALU.mult),
                    rstd, gr, free)
                o = Q.act(lambda e, k=k, t=t: e.activation(HT[:, k, 1:T + 1], t, ACT.Identity,
                                                           bias=modcol(1, 0, k)), o, fence)
                tmp_free[i] = o
                ht.append(o)
            xx_free = [None]

            def mix(n):
                ready = []
                for k in range(KT):
                    s = Q.pool(lambda e, k=k: e.tensor_tensor(XX[:, :], HT[:, k, 0:T], HT[:, k, 1:T + 1],
                                                              ALU.subtract), z, ht[k], xx_free[0])
                    i, t, free = tmp()
                    o = Q.dve(lambda e, k=k, t=t: e.scalar_tensor_tensor(
                        out=t, in0=XX[:, :], scalar=col("mu", 8 * n + k), in1=HT[:, k, 1:T + 1],
                        op0=ALU.mult, op1=ALU.add), s, free)
                    xx_free[0] = o
                    r = split_into(HH[:, k, :], HL[:, k, :], t, o, h_free[0])
                    tmp_free[i] = r
                    ready.append(r)
                return ready

            def lora(j, jobs, ready):
                wh, wl, cut = W.take(j)
                for c0, r0, fn, dst in jobs:
                    i, ps, free = big.get()
                    for k in range(KT):
                        for part, (a, b) in enumerate(((wh, HH), (wh, HL), (wl, HH))):
                            o = Q.pe(lambda e, a=a, b=b, k=k, c0=c0, part=part, ps=ps: e.matmul(
                                ps[:, :], a[:, k, c0:c0 + P], b[:, k, :], start=(k == 0 and part == 0),
                                stop=(k == KT - 1 and part == 2)), free, cut, ready[k])
                    r1 = P if r0 != 0 or dst is not WA else 64
                    r = Q.act(lambda e, r0=r0, r1=r1, ps=ps, fn=fn, dst=dst: e.activation(
                        dst[r0:r1, :], ps[r0:r1, :], fn), o)
                    big.done(i, r)
                W.used[j] = o
                h_free[0] = o
                return r

            WA, GA, GB = ADR[:, 0, :], ADR[:, 1, :], ADA[:, :]
            j = next_chunk()
            lora(j, [(0, 0, ACT.Tanh, WA)], mix(1))
            wa = lora(j, [(0, 64, ACT.Copy, WA)], mix(4))
            ga = lora(next_chunk(), [(0, 0, ACT.Sigmoid, GA), (32, 96, ACT.Sigmoid, GB)], mix(5))
            W.limit = len([1 for s in sched[:sched.index(("wo", 0))]])
            for dst, n in ((RR, 0), (KK, 2), (VV, 3)):
                def keep(m, ps, o, dst=dst):
                    return [Q.act(lambda e, ps=ps: e.activation(dst[:, m, :], ps[:, :], ACT.Copy), o)]
                h_free[0] = dense(4, HH, HL, mix(n), keep)

            fence = Q.last("pe", "act", "dve", "pool")
            at_ = [w_at]

            def scratch(name, shape):
                a = at_[0]
                at_[0] += 4 * int(np.prod(shape[1:]))
                return place(name, shape, F32, a)

            LO2 = scratch("LO2", [P, 3, D])
            TB2 = scratch("TB2", [P, 8, P])
            BK = scratch("BK", [P, 8, P])
            AR = scratch("AR", [P, 2, 8, P])
            GT = scratch("GT", [P, 2, 2, 8, P])
            BT = scratch("BT", [P, 2, 2, 8, 64])
            VS = scratch("VS", [P, 2, 2, 8, 64])
            LT = scratch("LT", [P, 8, P])
            TN = scratch("TN", [P, 8, P])
            UN = scratch("UN", [P, 8, P])
            assert at_[0] <= ar_at
            TT = place("TT", [P, 2, 8, P], F32, ar_at)
            TE = place("TE", [P, 4, T], F32, ar_at + 8192)
            SS = XX[:, 0:128]
            SE = XX[:, 128:256]
            X1 = XX[:, 256:320]
            EC = XX[:, 320:336].rearrange("p (b c) -> p b c", b=2)
            d_lo = Q.dma("sp", LO2[:, :, :], lo2, s_lo, 0, fence)
            d_tb = Q.dma("sp", TB2[:, :, :], tab[:, NMAIN:NTAB].rearrange("p (n c) -> p n c", c=P), s_lo, 1,
                         fence)
            d_lo = d_tb

            def tb2(name):
                return TB2[:, (TAB[name][0] - NMAIN) // P, :]

            zx = Q.pool(lambda e: e.memset(XX[:, :], 0.0), fence)
            T1, T2, T3, T5, T6, T0 = TE[:, 0, :], TE[:, 1, :], TE[:, 2, :], TE[:, 3, :], RST[:, :], ACC[:, :]
            F1, F2 = TMP[:, 0, :], TMP[:, 1, :]
            prep_b, inv_b = Banks(PS[0:4]), Banks(PS[4:6])
            PY, PC = PS[6], PS[7]
            state = {}
            first = [fence]
            tprev = {"bk": None, "lt": None, "elem": fence}
            hready = [None] * KT

            def h64(ap):
                return ap.rearrange("p (c t) -> p c t", t=64)

            def prep(m):
                b = m % 2
                st = state[m] = {}
                old = state.get(m - 2, {}).get("done")
                ms = slice(m * P, m * P + P)
                el = tprev["elem"]
                i, ps, free = prep_b.get()
                o = Q.pe(lambda e, ps=ps: e.matmul(ps[:, :], LO2[0:64, 0, ms], WA[0:64, :], start=True, stop=True),
                         d_lo, free, fence, wa)
                sg = Q.act(lambda e, ps=ps: e.activation(T0, ps[:, :], ACT.Sigmoid, bias=col("w0", m)), o, el)
                prep_b.done(i, sg)
                i, ps, free = prep_b.get()
                o = Q.pe(lambda e, ps=ps: e.matmul(ps[:, :], LO2[64:128, 0, ms], WA[64:128, :], start=True,
                                            stop=True), d_lo, free)
                ao = Q.act(lambda e, ps=ps: e.activation(T5, ps[:, :], ACT.Sigmoid, bias=col("a0", m)), o, el)
                prep_b.done(i, ao)
                kko = Q.dve(lambda e: e.tensor_scalar(T6, KK[:, m, :], col("k_k", m), None, ALU.mult), el)
                for c in range(8):
                    cs = slice(64 * c, 64 * c + 64)
                    so = Q.dve(lambda e, cs=cs: e.tensor_tensor_scan(T1[:, cs], tb("ones")[:, 0:64], T0[:, cs],
                                                                     0.0, ALU.mult, ALU.add), sg, el)
                cp = Q.dve(lambda e: e.tensor_tensor(T0, T1, T0, ALU.subtract), so)
                ep = Q.act(lambda e: e.activation(T2, T1, ACT.Exp, scale=-NE), so)
                em = Q.act(lambda e: e.activation(T3, T1, ACT.Exp, scale=NE), so)
                e0 = Q.act(lambda e: e.activation(T0, T0, ACT.Exp, scale=-NE), cp)
                sq = Q.act(lambda e: e.activation(T1, T6, ACT.Square), kko, cp, em)
                yield
                i, ps, free = prep_b.get()
                o = Q.pe(lambda e, ps=ps: e.matmul(ps[:, :], tb("bones"), T1, start=True, stop=True), sq, free)
                nr = Q.act(lambda e, ps=ps: e.activation(T1, ps[:, :], ACT.Sqrt), o)
                prep_b.done(i, nr)
                o = Q.dve(lambda e: e.tensor_scalar(T1, T1, 1e-12, None, ALU.max), nr)
                o = Q.dve(lambda e: e.reciprocal(T1, T1), o)
                kn = Q.dve(lambda e: e.tensor_tensor(T6, T6, T1, ALU.mult), o)
                o = Q.dve(lambda e: e.tensor_scalar(T1, T5, 1.0, col("k_a", m), ALU.subtract, ALU.mult), ao,
                          kn)
                k2 = Q.dve(lambda e: e.scalar_tensor_tensor(out=KK[:, m, :], in0=T1, scalar=1.0,
                                                            in1=KK[:, m, :], op0=ALU.add, op1=ALU.mult), o)
                aa = Q.dve(lambda e: e.scalar_tensor_tensor(out=AR[:, b, :, 0:64], in0=h64(T6), scalar=-1.0,
                                                            in1=h64(T0), op0=ALU.mult, op1=ALU.mult),
                           kn, e0, old)
                rr = Q.dve(lambda e: e.tensor_tensor(AR[:, b, :, 64:128], h64(RR[:, m, :]), h64(T2),
                                                     ALU.mult), ep, old)
                ec = Q.act(lambda e: e.activation(EC[:, b, :], h64(T2)[:, :, 63], ACT.Copy), ep, old, zx)
                o = Q.dve(lambda e: e.tensor_tensor(T5, T5, T6, ALU.mult), aa)
                for hh in range(2):
                    rows = slice(64 * hh, 64 * hh + 64)
                    ba, ka = (0, 64) if hh == 0 else (64, 0)
                    b1 = Q.dve(lambda e, rows=rows, ba=ba: e.tensor_tensor(
                        BK[rows, :, ba:ba + 64], h64(T5[rows]), h64(T3[rows]), ALU.mult), o, em, tprev["bk"])
                    b2 = Q.dve(lambda e, rows=rows, ka=ka: e.tensor_tensor(
                        BK[rows, :, ka:ka + 64], h64(KK[rows, m, :]), h64(T3[rows]), ALU.mult), k2)
                rk = Q.dve(lambda e: e.scalar_tensor_tensor(out=T1, in0=RR[:, m, :], scalar=col("r_k", m),
                                                            in1=KK[:, m, :], op0=ALU.mult, op1=ALU.mult), k2)
                tprev["elem"] = [rk, b2, ec]
                yield
                i, ps, free = prep_b.get()
                bo = Q.pe(lambda e, ps=ps: e.matmul(ps[:, :], tb("bones"), T1, start=True, stop=True), rk, free)
                tprev["elem"] = [rk, b2, ec, bo]
                bonus = Q.dve(lambda e, ps=ps: e.tensor_tensor(RR[:, m, :], ps[:, :], VV[:, m, :], ALU.mult), bo, rr)
                prep_b.done(i, bonus)
                gts = {}
                for half in range(2):
                    for hh in range(2):
                        rows = slice(64 * hh, 64 * hh + 64)
                        i, ps, free = prep_b.get()
                        for q in range(4):
                            c = 4 * half + q
                            o = Q.pe(lambda e, c=c, q=q, rows=rows, ps=ps: e.matmul(
                                ps[:, P * q:P * q + P], BK[rows, c, :], AR[rows, b, c, :], start=True,
                                stop=True), b1, b2, aa, rr, free)
                        mk = tb("rwm")[:, None, :].broadcast_to((P, 4, P))
                        g = Q.dve(lambda e, half=half, hh=hh, ps=ps, mk=mk: e.tensor_tensor(
                            GT[:, b, hh, 4 * half:4 * half + 4, :],
                            ps[:, :].rearrange("p (n c) -> p n c", c=P), mk, ALU.mult), o, old)
                        prep_b.done(i, g)
                        gts[hh] = g
                    yield
                bt = []
                for hh in range(2):
                    rows = slice(64 * hh, 64 * hh + 64)
                    i, ps, free = prep_b.get()
                    for c in range(8):
                        o = Q.pe(lambda e, c=c, rows=rows, ps=ps: e.transpose(
                            ps[:, 64 * c:64 * c + 64], BK[rows, c, :], tb("idk", rows)), free)
                    t_ = Q.act(lambda e, hh=hh, ps=ps: e.activation(BT[:, b, hh, :, :], h64(ps[:, :]),
                                                                    ACT.Copy), o, old)
                    prep_b.done(i, t_)
                    bt.append(t_)
                tprev["bk"] = o
                i, ps, free = prep_b.get()
                for c in range(8):
                    for hh in range(2):
                        o = Q.pe(lambda e, c=c, hh=hh, ps=ps: e.matmul(
                            ps[64 - 64 * hh:128 - 64 * hh, 64 * c:64 * c + 64],
                            VV[:, m, 64 * c:64 * c + 64], tb("ident")[:, 64 * hh:64 * hh + 64],
                            start=True, stop=True), free)
                vz = Q.pool(lambda e: e.memset(VS[:, b, :, :, :], 0.0), old, fence)
                for hh in range(2):
                    rows = slice(64 - 64 * hh, 128 - 64 * hh)
                    v = Q.act(lambda e, hh=hh, rows=rows, ps=ps: e.activation(
                        VS[rows, b, hh, :, :], h64(ps[rows, :]), ACT.Copy), o, vz)
                    bt.append(v)
                prep_b.done(i, v)
                vdone = [o, bonus]
                yield
                i, ps, free = prep_b.get()
                Q.pe(lambda e, ps=ps: e.matmul(ps[:, :], LO2[:, 1, ms], GA, start=True, stop=False), free, ga)
                o = Q.pe(lambda e, ps=ps: e.matmul(ps[:, :], LO2[96:128, 2, ms], GB[96:128, :], start=False,
                                            stop=True))
                go = Q.act(lambda e, ps=ps: e.activation(VV[:, m, :], ps[:, :], ACT.Copy), o, vdone)
                prep_b.done(i, go)
                l0 = Q.pool(lambda e: e.tensor_tensor(
                    LT[:, :, :].rearrange("p c (h t) -> p h c t", h=2), GT[:, b, :, :, 0:64],
                    tb("bones").rearrange("p (h t) -> p h t", h=2)[:, :, None, :].broadcast_to((P, 2, 8, 64)),
                    ALU.mult), gts[0], gts[1], tprev["lt"])
                mk = tb2("upp0")[:, None, :].broadcast_to((P, 8, P))
                idb = tb("ident")[:, None, :].broadcast_to((P, 8, P))
                o = Q.pool(lambda e: e.tensor_tensor(TT[:, b, :, :], LT[:, :, :], mk, ALU.mult), l0, old,
                           d_tb, fence)
                o = Q.pool(lambda e: e.tensor_tensor(TT[:, b, :, :], TT[:, b, :, :], idb, ALU.add), o)
                tto = None
                yield
                for v in inverse(LT[:, :, :], TT[:, b, :, :], TN[:, :, :], UN[:, :, :], tb2, 6, inv_b,
                                 [o, tprev["lt"]]):
                    if v:
                        tto = v
                    yield
                tprev["lt"] = Q.last("pe")
                st.update(pre=[aa, rr, gts[0], gts[1]] + bt, tt=tto, ec=ec, bonus=bonus, go=go)

            sfree = {"s": zx, "x1": None, "pc": None, "py": None, "f": Q.last("act", "dve")}

            def chain(m):
                b = m % 2
                st = state[m]
                s = Q.pool(lambda e: e.memset(SS, 0.0), sfree["s"])
                x1, pc = sfree["x1"], sfree["pc"]
                so = [s]
                ry = None
                for c in range(8):
                    se = Q.pool(lambda e, c=c: e.tensor_scalar(SE, SS, EC[:, b, c:c + 1], None, ALU.mult),
                                so, st["ec"])
                    for hh in range(2):
                        r = slice(64 * hh, 64 * hh + 64)
                        Q.pe(lambda e, r=r, c=c: e.matmul(PC[r, 0:64], AR[:, b, c, 0:64], SS[:, r],
                                                          start=True, stop=False), so, st["pre"], pc)
                        o = Q.pe(lambda e, r=r, c=c, hh=hh: e.matmul(
                            PC[r, 0:64], GT[:, b, hh, c, 0:64], VS[:, b, hh, c, :], start=False, stop=True))
                    ry = Q.pe(lambda e, c=c: e.matmul(PY[:, 64 * c:64 * c + 64], SS, AR[:, b, c, 64:128],
                                                      start=True, stop=False), sfree["py"])
                    xo = Q.dve(lambda e: e.tensor_copy(X1, PC[:, 0:64]), o, x1)
                    o = Q.pe(lambda e, c=c: e.matmul(PC[:, 64:128], TT[:, b, c, :], X1, start=True,
                                                     stop=True), xo, st["tt"], pc)
                    x1 = o
                    v0 = Q.act(lambda e, c=c: e.activation(VS[0:64, b, 0, c, :], PC[0:64, 64:128], ACT.Copy),
                               o)
                    v1 = Q.dve(lambda e, c=c: e.tensor_copy(VS[64:128, b, 1, c, :], PC[64:128, 64:128]), o)
                    if c % 2 == 1:
                        yield
                    for hh, vo in ((0, v0), (1, v1)):
                        r = slice(64 * hh, 64 * hh + 64)
                        o = Q.pe(lambda e, r=r, c=c, hh=hh: e.matmul(
                            PC[r, 128:192], BT[:, b, hh, c, :], VS[:, b, hh, c, :], start=True, stop=True),
                            vo)
                    for hh, vo in ((0, v0), (1, v1)):
                        r = slice(64 * hh, 64 * hh + 64)
                        yo = Q.pe(lambda e, r=r, c=c, hh=hh: e.matmul(
                            PY[r, 64 * c:64 * c + 64], VS[:, b, hh, c, :], GT[:, b, hh, c, 64:128],
                            start=False, stop=True))
                    so = []
                    for hh in range(2):
                        r = slice(64 * hh, 64 * hh + 64)
                        so.append(Q.dve(lambda e, r=r, c=c: e.scalar_tensor_tensor(
                            out=SS[r, r], in0=PC[r, 128:192], scalar=EC[r, b, c:c + 1], in1=SE[r, r],
                            op0=ALU.mult, op1=ALU.add), o, se, ry))
                    pc = so
                    yield
                sfree.update(s=[so, yo], x1=x1, pc=pc)
                st["done"] = [yo, so]
                y = KK[:, m, :]
                yc = Q.act(lambda e: e.activation(y, PY[:, :], ACT.Copy), yo)
                sfree["py"] = yc
                i, ps, free = sml_f.get()
                o = Q.pe(lambda e, ps=ps: e.matmul(ps[:, :], tb("bones"), y, start=True, stop=True), yc, free)
                o = Q.dve(lambda e, ps=ps: e.scalar_tensor_tensor(out=y, in0=ps[:, :], scalar=-1.0 / 64, in1=y,
                                                           op0=ALU.mult, op1=ALU.add), o)
                sml_f.done(i, o)
                q = Q.act(lambda e: e.activation(F1, y, ACT.Square), o, sfree["f"])
                yield
                i, ps, free = sml_f.get()
                o = Q.pe(lambda e, ps=ps: e.matmul(ps[:, :], tb("bones"), F1, start=True, stop=True), q, free)
                o = Q.dve(lambda e, ps=ps: e.tensor_scalar(F1, ps[:, :], 1.0 / 64, 64e-5, ALU.mult, ALU.add), o)
                sml_f.done(i, o)
                o = Q.act(lambda e: e.activation(F1, F1, ACT.Sqrt), o)
                o = Q.dve(lambda e: e.reciprocal(F1, F1), o)
                o = Q.dve(lambda e: e.scalar_tensor_tensor(out=y, in0=y, scalar=col("ln_w", m), in1=F1,
                                                           op0=ALU.mult, op1=ALU.mult), o)
                o = Q.dve(lambda e: e.scalar_tensor_tensor(out=y, in0=y, scalar=col("ln_b", m),
                                                           in1=RR[:, m, :], op0=ALU.add, op1=ALU.add), o,
                          st["bonus"])
                o = Q.dve(lambda e: e.tensor_tensor(y, y, VV[:, m, :], ALU.mult), o, st["go"])
                hready[m] = split_into(HH[:, m, :], HL[:, m, :], y, o, h_free[0])
                sfree["f"] = o
                yield

            sml_f = prep_b
            for _ in prep(0):
                pass
            for m in range(8):
                interleave(*([chain(m)] + ([prep(m + 1)] if m < 7 else [])))
            W.fence = Q.last("pe", "act", "dve", "pool")
            for bk in (big, sml):
                for i in range(4):
                    bk.done(i, *W.fence)
            tmp_free[0] = tmp_free[1] = W.fence
            rms_state["acc_free"] = rms_state["rst_free"] = W.fence
            W.limit = len(sched)
            gt = A.need(1, 2)
            last = dense(4, HH, HL, hready, residual(lambda m: modcol(1, 2, m), gt, True))
            h_free[0] = last
            for m in range(16):
                g_free[m] = Q.last("pe", "dve", "act", "pool")

        def swiglu(layer):
            base = 8 * layer
            ready = norm_split(lambda k: col("ffn_norm", base + k), d_cols, None, rms())
            final = layer == 1
            for g in range(2):
                gready = [None] * 16
                gate = {}

                def hidden(m, ps, o):
                    if m % 2 == 0:
                        i, t, free = tmp()
                        r = Q.act(lambda e, ps=ps: e.activation(t, ps[:, :], ACT.Silu), o, free)
                        gate[0] = (i, t, r)
                        return [r]
                    i, t, r = gate[0]
                    n = m // 2
                    r = Q.dve(lambda e, ps=ps: e.tensor_tensor(t, t, ps[:, :], ALU.mult), r, o)
                    h = split_into(GH[:, n, :], GL[:, n, :], t, r, g_free[n])
                    tmp_free[i] = h
                    gready[n] = h
                    return [r]

                h_free[0] = dense(11, HH, HL, ready, hidden)
                last = dense(8, GH, GL, gready, residual(None, None, g == 1 and not final))
                for m in range(16):
                    g_free[m] = last

        def gdn_mixer():
            rstd = rms()
            for k in range(KT):
                o = Q.dve(lambda e, k=k: e.scalar_tensor_tensor(
                    out=X[:, k, :], in0=X[:, k, :], scalar=col("final_g", k), in1=RST[:, :], op0=ALU.mult,
                    op1=ALU.mult), rstd)
                x_ready[k] = o
                square_add(k, o)
            rms_state["rst_free"] = o
            if stop == "fin":
                return
            ready = norm_split(lambda k: col("attn_norm", k), d_cols, None, rms())
            fence = Q.last("pe", "act", "dve", "pool")
            areas = [[ar_at + 16384, ar_at + 32768], [ar_at + 49152, ar_at + 67648]]

            def scratch(name, shape):
                size = (4 * int(np.prod(shape[1:])) + 31) // 32 * 32
                for a in areas:
                    if a[0] + size <= a[1]:
                        a[0] += size
                        return place(name, shape, F32, a[0] - size)
                raise MemoryError(name)

            TB2 = scratch("TG2", [P, 8, P])
            UU = scratch("UU", [P, 3, T + 3])
            ZZ = scratch("ZZ", [P, 2, T])
            QQ = scratch("QQ", [P, T])
            KG = scratch("KG", [P, T])
            VG = scratch("VG", [P, T])
            KB = scratch("KB", [P, T])
            DD = scratch("DD", [P, 4, P])
            LTg = scratch("LTg", [P, 4, P])
            TTg = scratch("TTg", [P, 4, P])
            TNg = scratch("TNg", [P, 4, P])
            UNg = scratch("UNg", [P, 4, P])
            AI = ADA[:, :].rearrange("p (c t) -> p c t", c=4)
            SG = scratch("SG", [P, P])
            GC = scratch("GC", [P, 80])
            US = ADR[:, 0, :].rearrange("p (c t) -> p c t", c=4)
            GG = ADR[:, 1, :]
            E1 = ADA[:, :]
            d_tb = Q.dma("sp", TB2[:, :, :], tab[:, NMAIN:NTAB].rearrange("p (n c) -> p n c", c=P), s_lo, 2,
                         fence)
            zu = Q.pool(lambda e: e.memset(UU[:, :, 0:3], 0.0), fence)

            def tb2(name):
                return TB2[:, (TAB[name][0] - NMAIN) // P, :]

            def ab(m, ps, o):
                be = Q.act(lambda e, ps=ps: e.activation(GG[32:40, :], ps[32:40, :], ACT.Sigmoid), o, fence)
                u = Q.dve(lambda e, ps=ps: e.tensor_scalar(E1[0:8, :], ps[0:8, :], col("dt_bias")[0:8], None,
                                                    ALU.add), o, fence, be)
                i, t, free = tmp()
                a = Q.act(lambda e: e.activation(t[0:8, :], E1[0:8, :], ACT.Abs), u, free)
                a = Q.act(lambda e: e.activation(t[0:8, :], t[0:8, :], ACT.Exp, scale=-1.0), a)
                a = Q.act(lambda e: e.activation(t[0:8, :], t[0:8, :], ACT.Ln, bias=1.0), a)
                n = Q.act(lambda e: e.activation(GC[0:8, 64:65], col("a_log")[0:8], ACT.Exp), fence, d_cols)
                a = Q.dve(lambda e: e.scalar_tensor_tensor(out=t[0:8, :], in0=E1[0:8, :], scalar=0.0,
                                                           in1=t[0:8, :], op0=ALU.max, op1=ALU.add), a)
                a = Q.dve(lambda e: e.tensor_scalar(t[0:8, :], t[0:8, :], GC[0:8, 64:65], -1.0, ALU.mult,
                                                    ALU.mult), a, n)
                for c in range(4):
                    cs = slice(P * c, P * c + P)
                    s = Q.dve(lambda e, cs=cs: e.tensor_tensor_scan(GG[0:8, cs], tb("ones")[0:8, :],
                                                                    t[0:8, cs], 0.0, ALU.mult, ALU.add),
                              a, fence)
                tmp_free[i] = s
                j, p2, free = sml.get()
                for c in range(4):
                    q = Q.pe(lambda e, c=c: e.transpose(p2[:, 8 * c:8 * c + 8], GG[0:8, P * c:P * c + P],
                                                        tb("ident")[0:8, 0:8]), s, free)
                g = Q.dve(lambda e: e.tensor_copy(GC[:, 0:32], p2[:, 0:32]), q, fence)
                sml.done(j, g)
                rows.extend([be, s, g])
                return [be, u]

            rows = []
            dense(1, HH, HL, ready, ab)

            taken = {"u": [zu] * 3, "z": [fence, fence], "all": fence}
            raw = {}
            hready = [None] * KT
            DK = P ** -0.5

            def project(h):
                raw[h] = {}
                for n in range(2):
                    j = next_chunk()
                    wh, wl, cut = W.take(j)
                    for c0 in (0, P):
                        r = 2 * n + c0 // P
                        i, ps, free = big.get()
                        for k in range(KT):
                            for part, (a, b) in enumerate(((wh, HH), (wh, HL), (wl, HH))):
                                o = Q.pe(lambda e, ps=ps, a=a, b=b, k=k, c0=c0, part=part: e.matmul(
                                    ps[:, :], a[:, k, c0:c0 + P], b[:, k, :], start=(k == 0 and part == 0),
                                    stop=(k == KT - 1 and part == 2)), free, cut, ready[k])
                        if r < 3:
                            t = Q.act(lambda e, r=r, ps=ps: e.activation(UU[:, r, 3:T + 3], ps[:, :],
                                                                         ACT.Copy), o, taken["u"][r])
                        else:
                            t = Q.act(lambda e, ps=ps: e.activation(ZZ[:, h % 2, :], ps[:, :], ACT.Silu), o,
                                      taken["z"][h % 2])
                        big.done(i, t)
                        raw[h][r] = t
                        if c0:
                            W.used[j] = o
                        yield
                h_free[0] = o

            def head(h):
                before = taken["all"]
                dst = (QQ, KG, VG)
                cv = []
                for r in range(3):
                    w0 = 8 * r + h
                    a = Q.dve(lambda e, r=r, w0=w0: e.tensor_scalar(
                        dst[r][:, :], UU[:, r, 0:T], col("gconv", w0), None, ALU.mult), raw[h][r], before,
                        zu)
                    for j in range(1, 4):
                        a = Q.dve(lambda e, r=r, j=j, w0=w0: e.scalar_tensor_tensor(
                            out=dst[r][:, :], in0=UU[:, r, j:j + T], scalar=col("gconv", 24 * j + w0),
                            in1=dst[r][:, :], op0=ALU.mult, op1=ALU.add), a)
                    taken["u"][r] = a
                    a = Q.act(lambda e, r=r: e.activation(dst[r][:, :], dst[r][:, :], ACT.Silu), a)
                    cv.append(a)
                    yield
                nrm = []
                for r in range(2):
                    i, t, free = tmp()
                    a = Q.act(lambda e, r=r, t=t: e.activation(t, dst[r][:, :], ACT.Square), cv[r], free)
                    j, ps, pf = sml.get()
                    o = Q.pe(lambda e, t=t, ps=ps: e.matmul(ps[:, :], tb("ones"), t, start=True, stop=True),
                             a, pf)
                    a = Q.dve(lambda e, t=t, ps=ps: e.tensor_scalar(t, ps[:, :], 1e-6, None, ALU.add), o)
                    sml.done(j, a)
                    a = Q.act(lambda e, t=t: e.activation(t, t, ACT.Sqrt), a)
                    a = Q.dve(lambda e, t=t: e.reciprocal(t, t), a)
                    a = Q.dve(lambda e, r=r, t=t: e.scalar_tensor_tensor(
                        out=dst[r][:, :], in0=dst[r][:, :], scalar=DK if r == 0 else 1.0, in1=t,
                        op0=ALU.mult, op1=ALU.mult), a)
                    tmp_free[i] = a
                    nrm.append(a)
                    yield
                j, pb_, pf = sml.get()
                o = Q.pe(lambda e: e.matmul(pb_[:, :], tb("ident")[32:40, 32 + h:33 + h].broadcast_to((8, P)),
                                            GG[32:40, :], start=True, stop=True), rows, pf)
                kb = Q.dve(lambda e: e.tensor_tensor(KB[:, :], KG[:, :], pb_[:, :], ALU.mult), o, nrm)
                vb = Q.dve(lambda e: e.tensor_tensor(VG[:, :], VG[:, :], pb_[:, :], ALU.mult), cv)
                sml.done(j, vb)
                j, pg, pf = sml.get()
                o = Q.pe(lambda e: e.matmul(pg[:, :], tb("ident")[0:8, h:h + 1].broadcast_to((8, P)),
                                            GG[0:8, :], start=True, stop=True), rows, pf)
                for c in range(4):
                    d = Q.dve(lambda e, c=c: e.tensor_scalar(
                        DD[:, c, :], pg[:, P * c:P * c + P], GC[:, 8 * c + h:8 * c + h + 1], 0.0,
                        ALU.subtract, ALU.min), o, before)
                gl = Q.dve(lambda e: e.tensor_copy(
                    GC[:, 40:44], pg[:, :].rearrange("p (c t) -> p c t", c=4)[:, :, 127]), o, before)
                i1, t1, f1 = tmp()
                i2, t2, f2 = tmp()
                eg = Q.act(lambda e: e.activation(t1, pg[:, :], ACT.Exp), o, f1, gl)
                for c in range(4):
                    ek = Q.act(lambda e, c=c: e.activation(t2[:, P * c:P * c + P], pg[:, P * c:P * c + P],
                                                           ACT.Exp, scale=-1.0, bias=GC[:, 40 + c:41 + c]),
                               gl, f2)
                dd = Q.act(lambda e: e.activation(DD[:, :, :], DD[:, :, :], ACT.Exp), d)
                egl = Q.act(lambda e: e.activation(GC[:, 48:52], GC[:, 40:44], ACT.Exp), gl)
                sml.done(j, ek, eg, d, gl)
                yield
                j1, p1, pf1 = sml.get()
                for c in range(4):
                    cs = slice(P * c, P * c + P)
                    o1 = Q.pe(lambda e, cs=cs: e.matmul(p1[:, cs], KG[:, cs], KB[:, cs], start=True,
                                                        stop=True), kb, pf1)
                j2, p2, pf2 = sml.get()
                for c in range(4):
                    cs = slice(P * c, P * c + P)
                    o2 = Q.pe(lambda e, cs=cs: e.matmul(p2[:, cs], KG[:, cs], QQ[:, cs], start=True,
                                                        stop=True), nrm, pf2)
                v4 = lambda p_: p_[:, :].rearrange("p (c t) -> p c t", c=4)
                bc = lambda name: tb(name)[:, None, :].broadcast_to((P, 4, P))
                l = Q.dve(lambda e: e.scalar_tensor_tensor(out=LTg[:, :, :], in0=v4(p1), scalar=-1.0,
                                                           in1=DD[:, :, :], op0=ALU.mult, op1=ALU.mult),
                          o1, dd, before)
                sml.done(j1, l)
                ai = Q.dve(lambda e: e.tensor_tensor(AI[:, :, :], v4(p2), DD[:, :, :], ALU.mult), o2, rows)
                sml.done(j2, ai)
                l = Q.pool(lambda e: e.tensor_tensor(LTg[:, :, :], LTg[:, :, :], bc("sup"), ALU.mult), l)
                m2 = tb2("upp0")[:, None, :].broadcast_to((P, 4, P))
                t0 = Q.pool(lambda e: e.tensor_tensor(TTg[:, :, :], LTg[:, :, :], m2, ALU.mult), l, d_tb,
                            before)
                t0 = Q.pool(lambda e: e.tensor_tensor(TTg[:, :, :], TTg[:, :, :], bc("ident"), ALU.add), t0)
                ai = Q.pool(lambda e: e.tensor_tensor(AI[:, :, :], AI[:, :, :], bc("supi"), ALU.mult), ai)
                qd = Q.dve(lambda e: e.tensor_tensor(QQ[:, :], QQ[:, :], t1, ALU.mult), eg, o2)
                ke = Q.dve(lambda e: e.tensor_tensor(KB[:, :], KB[:, :], t1, ALU.mult), eg, o1)
                kd = Q.dve(lambda e: e.tensor_tensor(KG[:, :], KG[:, :], t2, ALU.mult), ek, o1, o2)
                tmp_free[i1], tmp_free[i2] = ke, kd
                yield
                tto = None
                for v in inverse(LTg[:, :, :], TTg[:, :, :], TNg[:, :, :], UNg[:, :, :], tb2, 7, sml,
                                 [t0, before]):
                    if v:
                        tto = v
                    yield
                inv = Q.last("pe", "dve")
                XK, XV, KD, WT = TNg, UNg, DD, KB[:, :].rearrange("p (c t) -> p c t", c=4)
                tk = []
                for src, dstt, w_ in ((KB, XK, ke), (VG, XV, vb), (KG, KD, kd)):
                    j, ps, pf = sml.get()
                    for c in range(4):
                        cs = slice(P * c, P * c + P)
                        o = Q.pe(lambda e, cs=cs, src=src, ps=ps: e.transpose(ps[:, cs], src[:, cs],
                                                                              tb("ident")), w_, pf)
                    a = Q.act(lambda e, ps=ps, dstt=dstt: e.activation(dstt[:, :, :], v4(ps), ACT.Copy), o,
                              inv, l, ai)
                    sml.done(j, a)
                    tk.append(a)
                yield
                j, ps, pf = sml.get()
                for c in range(4):
                    o = Q.pe(lambda e, c=c, ps=ps: e.matmul(ps[:, P * c:P * c + P], TTg[:, c, :],
                                                            XV[:, c, :], start=True, stop=True), tto, tk, pf)
                us = Q.dve(lambda e, ps=ps: e.tensor_copy(US, v4(ps)), o, before)
                sml.done(j, us)
                j, ps, pf = sml.get()
                for c in range(1, 4):
                    o = Q.pe(lambda e, c=c, ps=ps: e.matmul(ps[:, P * c:P * c + P], XK[:, c, :],
                                                            TTg[:, c, :], start=True, stop=True), pf)
                wt = Q.act(lambda e, ps=ps: e.activation(WT[:, 1:4, :], v4(ps)[:, 1:4, :], ACT.Copy), o, tk)
                sml.done(j, wt)
                yield
                jo, po, pfo = sml.get()
                s = None
                for c in range(4):
                    cs = slice(P * c, P * c + P)
                    vn = us
                    if c:
                        j, ps, pf = sml.get()
                        o = Q.pe(lambda e, c=c, ps=ps: e.matmul(ps[:, 0:P], WT[:, c, :], SG[:, :],
                                                                start=True, stop=True), wt, s, pf)
                        vn = Q.dve(lambda e, c=c, ps=ps: e.tensor_tensor(US[:, c, :], US[:, c, :],
                                                                         ps[:, 0:P], ALU.subtract), o)
                        sml.done(j, vn)
                        Q.pe(lambda e, cs=cs: e.matmul(po[:, cs], SG[:, :], QQ[:, cs], start=True,
                                                       stop=False), qd, s, pfo)
                    oo = Q.pe(lambda e, cs=cs, c=c: e.matmul(po[:, cs], US[:, c, :], AI[:, c, :],
                                                             start=(c == 0), stop=True), vn, ai, pfo)
                    if c < 3:
                        j, ps, pf = sml.get()
                        if j == jo:
                            j, ps, pf = sml.get()
                        o = Q.pe(lambda e, c=c, ps=ps: e.matmul(ps[:, 0:P], KD[:, c, :], US[:, c, :],
                                                                start=True, stop=True), vn, tk, pf)
                        if c == 0:
                            s = Q.dve(lambda e, ps=ps: e.tensor_copy(SG[:, :], ps[:, 0:P]), o, before)
                        else:
                            s = Q.dve(lambda e, c=c, ps=ps: e.scalar_tensor_tensor(
                                out=SG[:, :], in0=SG[:, :], scalar=GC[:, 48 + c:49 + c], in1=ps[:, 0:P],
                                op0=ALU.mult, op1=ALU.add), o, egl, oo)
                        sml.done(j, s)
                    if c < 3:
                        while sml.n % 4 == jo:
                            sml.n += 1
                        yield
                i, t, free = tmp()
                a = Q.act(lambda e: e.activation(t, po[:, :], ACT.Square), oo, free)
                oc = Q.dve(lambda e: e.tensor_scalar(QQ[:, :], po[:, :], col("o_gain"), None, ALU.mult), oo, a)
                sml.done(jo, a, oc)
                j, ps, pf = sml.get()
                o = Q.pe(lambda e, ps=ps: e.matmul(ps[:, :], tb("ones"), t, start=True, stop=True), a, pf)
                a = Q.dve(lambda e, ps=ps: e.tensor_scalar(t, ps[:, :], 1.0 / P, 1e-6, ALU.mult, ALU.add), o)
                sml.done(j, a)
                a = Q.act(lambda e: e.activation(t, t, ACT.Sqrt), a)
                a = Q.dve(lambda e: e.reciprocal(t, t), a)
                a = Q.dve(lambda e: e.tensor_tensor(t, t, ZZ[:, h % 2, :], ALU.mult), a, raw[h][3])
                taken["z"][h % 2] = a
                a = Q.dve(lambda e: e.tensor_tensor(t, t, QQ[:, :], ALU.mult), a, oc)
                hready[h] = split_into(GH[:, h, :], GL[:, h, :], t, a, [g_free[h], fence])
                tmp_free[i] = hready[h]
                taken["all"] = [oo, o] + Q.last("dve", "act", "pool", "pe")
                yield

            for _ in project(0):
                pass
            for h in range(8):
                interleave(*([head(h)] + ([project(h + 1)] if h < 7 else [])))
            last = dense(4, GH, GL, hready, residual(None, None, True))
            for m in range(16):
                g_free[m] = Q.last("pe", "dve", "act", "pool")

        def sb_mixer():
            rstd = rms()
            KS = place("KS", [P, 8, T], F32, ar_at)
            VT = place("VT", [P, 4, D], F32, ar_at + 16384)
            QS = place("QS", [P, 8, T], F32, ar_at + 32768)
            fence = Q.last("pe", "act", "dve", "pool")
            SCALE = P ** -0.5

            def heads(dst, gname, ready_to):
                def consume(m, ps, o):
                    i, t, free = tmp()
                    a = Q.act(lambda e, ps=ps: e.activation(t, ps[:, :], ACT.Square), o, free)
                    g = Q.dve(lambda e, ps=ps: e.tensor_scalar(dst[:, m, :], ps[:, :], col(gname), None, ALU.mult),
                              o, fence, a)
                    j, p2, pf = sml.get()
                    q = Q.pe(lambda e: e.matmul(p2[:, :], tb("ones"), t, start=True, stop=True), a, pf)
                    b = Q.dve(lambda e: e.tensor_scalar(t, p2[:, :], 1.0 / P, 1e-6, ALU.mult, ALU.add), q)
                    sml.done(j, b)
                    b = Q.act(lambda e: e.activation(t, t, ACT.Sqrt), b)
                    b = Q.dve(lambda e: e.reciprocal(t, t), b)
                    b = Q.dve(lambda e: e.tensor_tensor(dst[:, m, :], dst[:, m, :], t, ALU.mult), b, g)
                    tmp_free[i] = b
                    ready_to[m] = b
                    return [a, g]
                return consume

            kr, qr, vr = [None] * 8, [None] * 8, [None] * 4
            ready = norm_split(lambda k: col("kv_norm", k), d_cols, None, rstd)
            dense(4, HH, HL, ready, heads(KS, "k_gain", kr))
            for n in range(4):
                j = next_chunk()
                wh, wl, cut = W.take(j)
                for tbk in range(4):
                    i, ps, free = big.get()
                    ts = slice(P * tbk, P * tbk + P)
                    for k in range(KT):
                        for part, (a, b) in enumerate(((wh, HH), (wh, HL), (wl, HH))):
                            o = Q.pe(lambda e, ps=ps, a=a, b=b, k=k, ts=ts, part=part: e.matmul(
                                ps[:, 0:256], b[:, k, ts], a[:, k, :], start=(k == 0 and part == 0),
                                stop=(k == KT - 1 and part == 2)), free, cut, ready[k])
                    v = Q.act(lambda e, ps=ps, tbk=tbk, n=n: e.activation(
                        VT[:, tbk, 256 * n:256 * n + 256], ps[:, 0:256], ACT.Copy), o, fence)
                    big.done(i, v)
                vr[n] = v
                W.used[j] = o
            h_free[0] = o
            ready = norm_split(lambda k: col("attn_norm", 8 + k), d_cols, None, rstd)
            h_free[0] = dense(4, HH, HL, ready, heads(QS, "q_gain", qr))

            LF = place("LF", [P, 2, 1280], F32, ar_at + 49152)
            ZS = place("ZS", [P, 2, T], F32, ar_at + 49152 + 10240)
            AT = place("AT", [P, 2, T], F32, ar_at + 49152 + 14336)
            off = [0, 512, 896, 1152]
            hready = [None] * KT
            lf_free, zs_free, at_free = [None, None], [None, None], [None, None]
            zb, rb, ob = Banks(PS[0:3]), Banks(PS[3:6]), Banks(PS[6:8])
            for bk in (zb, rb, ob):
                for i in range(len(bk.tiles)):
                    bk.done(i, *Q.last("act", "dve"))

            def attend(h):
                b = h % 2
                jo, po, pfo = ob.get()
                lf = {}
                for j in (3, 2, 1, 0):
                    w_ = T - P * j
                    L = LF[:, b, off[j]:off[j] + w_]
                    Z = ZS[:, b, 0:w_]
                    Aw = AT[:, b, 0:w_]
                    i, ps, pf = zb.get()
                    o = Q.pe(lambda e, ps=ps, j=j, w_=w_: e.matmul(
                        ps[:, 0:w_], KS[:, h, P * j:P * j + P], QS[:, h, P * j:T], start=True, stop=True),
                        kr, qr, pf)
                    z = Q.act(lambda e, ps=ps, w_=w_, Z=Z: e.activation(Z, ps[:, 0:w_], ACT.Identity,
                                                                        scale=SCALE), o, zs_free[b], fence)
                    a = Q.act(lambda e, ps=ps, w_=w_, L=L: e.activation(L, ps[:, 0:w_], ACT.Abs,
                                                                        scale=SCALE), o, lf_free[b], fence)
                    zb.done(i, z, a)
                    a = Q.act(lambda e, L=L: e.activation(L, L, ACT.Exp, scale=-1.0), a)
                    a = Q.act(lambda e, L=L: e.activation(L, L, ACT.Ln, bias=1.0), a)
                    a = Q.dve(lambda e, L=L, Z=Z: e.scalar_tensor_tensor(out=L, in0=Z, scalar=0.0, in1=L,
                                                                         op0=ALU.max, op1=ALU.add), a, z)
                    zm = Q.pool(lambda e, Z=Z: e.tensor_tensor(Z[:, 0:P], Z[:, 0:P], tb("sup"), ALU.mult), a)
                    lf[j] = Q.pool(lambda e, L=L: e.tensor_tensor(L[:, 0:P], L[:, 0:P], tb("sup"),
                                                                  ALU.mult), a)
                    yield
                    i, pr, pf = rb.get()
                    for j2 in range(j, 4):
                        w2 = T - P * j2
                        o = Q.pe(lambda e, pr=pr, j=j, j2=j2, w2=w2, w_=w_: e.matmul(
                            pr[:, w_ - w2:w_], tb("tri" if j2 == j else "ones"),
                            LF[:, b, off[j2]:off[j2] + w2], start=(j2 == j), stop=(j2 == 3)),
                            lf[j2], pf)
                    lo_ = o
                    d = Q.dve(lambda e, pr=pr, w_=w_, Z=Z, Aw=Aw: e.scalar_tensor_tensor(
                        out=Aw, in0=pr[:, 0:w_], scalar=-1.0, in1=Z, op0=ALU.mult, op1=ALU.add), o, zm,
                        at_free[b])
                    rb.done(i, d)
                    zs_free[b] = d
                    d = Q.act(lambda e, Aw=Aw: e.activation(Aw, Aw, ACT.Exp), d)
                    d = Q.pool(lambda e, Aw=Aw: e.tensor_tensor(Aw[:, 0:P], Aw[:, 0:P], tb("sup"),
                                                                ALU.mult), d)
                    o = Q.pe(lambda e, j=j, Aw=Aw: e.matmul(
                        po[:, P * j:T], VT[:, j, P * h:P * h + P], Aw, start=(j == 3), stop=(j == 0),
                        skip_group_check=True), d, vr, pfo)
                    at_free[b] = o
                    yield
                lf_free[b] = lo_
                hi = Q.act(lambda e: e.activation(HH[:, h, :], po[:, :], ACT.Copy), o, h_free[0])
                lo = Q.dve(lambda e: e.tensor_tensor(HL[:, h, :], po[:, :], HH[:, h, :].bitcast(F32),
                                                     ALU.subtract), hi)
                hready[h] = [hi, lo]
                ob.done(jo, hi, lo)

            for h in range(0, 8, 2):
                interleave(attend(h), attend(h + 1))
            end = Q.last("act", "dve")
            for bk in (big, sml):
                for i in range(4):
                    bk.done(i, *end)
            h_free[0] = dense(4, HH, HL, hready, residual(None, None, True))
            for m in range(16):
                g_free[m] = Q.last("pe", "dve", "act", "pool")

        def whole():
            conv_mixer()
            if stop == "conv":
                return
            mlp(0)
            if stop == "mlp0":
                return
            rwkv_mixer()
            if stop == "rwkv":
                return
            mlp(1)
            if stop == "mlp1":
                return
            gdn_mixer()
            if stop in ("fin", "gdn"):
                return
            swiglu(0)
            if stop == "ffn0":
                return
            sb_mixer()
            if stop == "sb":
                return
            swiglu(1)

        whole()
        finish()
        Q.number()
        block = ctx.enter_context(nc.Block())

        @block.sync
        def _(e):
            Q.emit("sp", e)
            e.wait_ge(s_out, 16)

        @block.scalar
        def _(e):
            Q.emit("act", e)

        @block.vector
        def _(e):
            Q.emit("dve", e)

        @block.gpsimd
        def _(e):
            Q.emit("pool", e)

        @block.tensor
        def _(e):
            Q.emit("pe", e)


def layout(inputs):
    def vec(a):
        return np.asarray(a).reshape(-1, P).T

    def chunks(a, c=256):
        a = np.asarray(a)
        k, n = a.shape
        return np.ascontiguousarray(a.reshape(k // P, P, n // c, c).transpose(2, 1, 0, 3)).reshape(n // c, P, -1)

    def rowpad(a):
        z = np.zeros((P, 1), np.float32)
        z[:a.shape[0], 0] = a
        return z

    g = {k: np.asarray(v) for k, v in inputs.items()}
    cols = {
        "c": vec(g["c"]), "norm_g": vec(g["norm_g"]), "final_g": vec(g["final_g"]), "ada_b": vec(g["ada_b"]),
        "conv_w": vec(g["conv_w"]), "mu": vec(g["rw_mu"]), "w0": vec(g["rw_w0"]), "a0": vec(g["rw_a0"]),
        "k_k": vec(g["rw_k_k"]), "k_a": vec(g["rw_k_a"]), "r_k": vec(g["rw_r_k"]), "ln_w": vec(g["rw_ln_w"]),
        "ln_b": vec(g["rw_ln_b"]), "attn_norm": vec(g["attn_norm_2"]), "ffn_norm": vec(g["ffn_norm_2"]),
        "kv_norm": vec(g["kv_norm_2"]), "gconv": vec(g["gdn_conv_w_2"]), "o_gain": vec(g["gdn_o_gain_2"]),
        "k_gain": vec(g["k_gain_2"]), "q_gain": vec(g["sb_q_gain_2"]), "a_log": rowpad(g["gdn_a_log_2"][0]),
        "dt_bias": rowpad(g["gdn_dt_bias_2"][0]),
    }
    packed = np.concatenate([cols[n] for n in COLS], axis=1).astype(np.float32, copy=False)
    ada = g["ada_w"].reshape(2, 8, P, 12, 512).transpose(0, 3, 1, 2, 4).reshape(192, P, 512)

    def cat(*a):
        return np.concatenate(a, axis=0)

    cin = g["conv_w_in"][0]
    parts = []
    for q in range(4):
        a, b = 256 * q, 256 * q + P
        for f in (a, b):
            parts += [cin[:, 1024 + f:1024 + f + P], cin[:, 2048 + f:2048 + f + P]]
        parts.append(cin[:, a:a + 256])
    rkv = g["rw_w_rkv"][0]
    gin = g["gdn_w_in_2"][0]
    n = QKVZ = 4096
    gab = np.concatenate([gin[:, n + 8:n + 16], gin[:, 0:24], gin[:, n:n + 8], gin[:, 0:88]], axis=1)
    heads = []
    for h in range(8):
        heads += [gin[:, j * 1024 + h * P:j * 1024 + h * P + P] for j in range(4)]

    def gu(a):
        f = a.shape[1] // 2
        return chunks(np.concatenate([a[:, s + i * P:s + i * P + P] for i in range(22) for s in (0, f)], axis=1))

    def m2(a, n):
        return cat(*[chunks(a[i * n * P:(i + 1) * n * P], P) for i in range(2)])

    w = {
        "cin": chunks(np.concatenate(parts, axis=1)), "cout": chunks(g["conv_w_out"][0]),
        "m1": cat(*[chunks(a) for a in g["mlp_w1"]]), "m2": cat(*[m2(a, 16) for a in g["mlp_w2"]]),
        "lwa": chunks(np.concatenate([g["rw_w1"][0], g["rw_a1"][0]], axis=1), 128),
        "lg": chunks(g["rw_g1"][0], 160),
        "rkv": cat(*[chunks(a) for a in rkv]), "wo": chunks(g["rw_w_o"][0]),
        "gab": chunks(gab, 128), "gin": chunks(np.concatenate(heads, axis=1)), "gout": chunks(g["gdn_w_out_2"][0]),
        "kv": chunks(g["w_kv_2"]), "sq": chunks(g["sb_w_q_2"][0]), "so": chunks(g["sb_w_out_2"][0]),
        "gu": cat(*[gu(a) for a in g["ffn_w_gu_2"]]), "dn": cat(*[m2(a, 11) for a in g["ffn_w_down_2"]]),
    }
    g2 = g["rw_g2"][0]
    lo2 = np.stack([cat(g["rw_w2"][0], g["rw_a2"][0]), g2[0:128], cat(g2[64:160], g2[128:160])], axis=1)
    return {
        "x": g["x"][0].T.reshape(KT, P, T).transpose(1, 0, 2), "cols": packed, "tab": tables(), "ada": ada,
        "lo2": lo2, **{"w_" + k: v for k, v in w.items()},
    }


def kernel(**inputs):
    import concourse.bacc as bacc
    from concourse.bass_utils import run_bass_kernel_spmd

    nc = bacc.Bacc("TRN2", target_bir_lowering=False, num_devices=1)
    arrays = {k: np.ascontiguousarray(v) for k, v in layout(inputs).items()}
    t = {k: nc.dram_tensor(k, v.shape, F32, kind="ExternalInput").ap() for k, v in arrays.items()}
    out = nc.dram_tensor("out", (P, KT, T), F32, kind="ExternalOutput").ap()
    build(nc, t["x"], t["cols"], t["tab"], t["ada"], {k: t["w_" + k] for k in STREAM}, t["lo2"], out)
    r = run_bass_kernel_spmd(nc, [arrays], core_ids=[0])
    y = r.results[0]["out"]
    return np.ascontiguousarray(y.transpose(1, 0, 2).reshape(D, T).T).reshape(1, T, D)
```

```python
from contextlib import ExitStack

import numpy as np
import concourse.bass as bass
from concourse import mybir
from concourse.alu_op_type import AluOpType as ALU

F32 = mybir.dt.float32
F32R = mybir.dt.float32r
ACT = mybir.ActivationFunctionType

P = 128
T = 512
KT = 8
D = 1024

COLS = {}


def _cols():
    at = 0
    for name, n in [("c", 8), ("norm_g", 32), ("final_g", 8), ("ada_b", 96), ("conv_w", 24), ("mu", 48),
                    ("w0", 8), ("a0", 8), ("k_k", 8), ("k_a", 8), ("r_k", 8), ("ln_w", 8), ("ln_b", 8),
                    ("attn_norm", 16), ("ffn_norm", 16), ("kv_norm", 8), ("gconv", 96),
                    ("o_gain", 1), ("k_gain", 1), ("q_gain", 1), ("a_log", 1), ("dt_bias", 1)]:
        COLS[name] = (at, n)
        at += n
    return at


NCOL = _cols()

TAB = {}
NMAIN = 7 * P + 66


def tables():
    i = np.arange(P)[:, None]
    j = np.arange(P)[None, :]
    parts = []

    def put(name, a):
        TAB[name] = (sum(x.shape[1] for x in parts), a.shape[1])
        parts.append(np.ascontiguousarray(np.broadcast_to(a, (P, a.shape[1])), dtype=np.float32))

    put("ones", np.ones((P, P)))
    put("ident", (i == j))
    put("bones", (i // 64 == j // 64))
    put("tri", (i >= j))
    put("sup", (i < j))
    put("supi", (i <= j))
    put("rwm", np.concatenate([(i % 64 < j[:, :64]), (i % 64 <= j[:, :64])], axis=1))
    put("idk", np.concatenate([np.eye(64), np.eye(64)], axis=0))
    put("eps", np.array([[1e-6, 64e-5]]))
    for n in range(7):
        m = 1 << n
        put(f"low{n}", (i // (2 * m) == j // (2 * m)) & (i % (2 * m) >= m) & (j % (2 * m) < m))
    put("upp0", (i // 2 == j // 2) & (i < j))
    return np.concatenate(parts, axis=1)


NTAB = tables().shape[1]

STREAM = {
    "cin": (12, 8, 256), "cout": (4, 8, 256), "m1": (32, 8, 256), "m2": (32, 16, 128),
    "lwa": (1, 8, 128), "lg": (1, 8, 160), "rkv": (12, 8, 256), "wo": (4, 8, 256),
    "gab": (1, 8, 128), "gin": (16, 8, 256), "gout": (4, 8, 256), "kv": (8, 8, 256), "sq": (4, 8, 256),
    "so": (4, 8, 256), "gu": (44, 8, 256), "dn": (32, 11, 128), "ada": (48, 4, 512),
}


def order():
    out = []

    def add(name, a, b):
        out.extend((name, i) for i in range(a, b))

    def mlp(layer):
        for g in range(2):
            add("m1", 16 * layer + 8 * g, 16 * layer + 8 * g + 8)
            add("m2", 16 * layer + 8 * g, 16 * layer + 8 * g + 8)

    def ffn(layer):
        for g in range(2):
            add("gu", 22 * layer + 11 * g, 22 * layer + 11 * g + 11)
            add("dn", 16 * layer + 8 * g, 16 * layer + 8 * g + 8)

    add("cin", 0, 12)
    add("cout", 0, 4)
    mlp(0)
    for i in range(40):
        out.insert(2 * i + 1, ("ada", 8 + i))
    add("lwa", 0, 1)
    add("lg", 0, 1)
    add("rkv", 0, 12)
    add("wo", 0, 4)
    mlp(1)
    add("gab", 0, 1)
    add("gin", 0, 16)
    add("gout", 0, 4)
    ffn(0)
    add("kv", 0, 8)
    add("sq", 0, 4)
    add("so", 0, 4)
    ffn(1)
    return out


class Op:

    def __init__(self, eng, fn, waits):
        self.eng, self.fn, self.waits = eng, fn, waits
        self.used, self.val, self.quiet = False, 0, False


class Dma:

    def __init__(self, sem, val):
        self.sem, self.val = sem, val


class Queues:

    def __init__(self, nc, ctx):
        self.nc = nc
        self.q = {e: [] for e in ("pe", "act", "dve", "pool", "sp")}
        self.sem = {e: ctx.enter_context(nc.semaphore("s_" + e)) for e in ("pe", "act", "dve", "pool")}
        self.ctx = ctx
        self.stores = []

    def add(self, eng, fn, waits):
        flat = []

        def walk(w):
            if w is None:
                return
            if isinstance(w, (list, tuple)):
                for x in w:
                    walk(x)
            else:
                flat.append(w)
                if isinstance(w, Op):
                    w.used = True

        walk(waits)
        op = Op(eng, fn, flat)
        self.q[eng].append(op)
        return op

    def pe(self, fn, *w):
        return self.add("pe", fn, w)

    def act(self, fn, *w):
        return self.add("act", fn, w)

    def dve(self, fn, *w):
        return self.add("dve", fn, w)

    def pool(self, fn, *w):
        return self.add("pool", fn, w)

    def dma(self, eng, dst, src, sem, count, *w):
        self.add(eng, lambda e: e.dma_start(dst, src).then_inc(sem, 16), w)
        return Dma(sem, 16 * (count + 1))

    def last(self, *engs):
        out = []
        for e in engs:
            ops = [op for op in self.q[e][-2:] if not op.quiet]
            out.extend(ops[-1:])
        return out

    def table(self, name):
        self.add("act", lambda e: e.preload_act_table_set(name), ()).quiet = True

    def emit(self, eng, e):
        n, seen = 0, {}
        for op in self.q[eng]:
            need = {}
            for w in op.waits:
                sem, val = (self.sem[w.eng], w.val) if isinstance(w, Op) else (w.sem, w.val)
                key = sem.name
                if val > seen.get(key, 0) and val > need.get(key, (None, 0))[1]:
                    need[key] = (sem, val)
            for key, (sem, val) in need.items():
                e.wait_ge(sem, val)
                seen[key] = val
            ins = op.fn(e)
            if op.used:
                ins.then_inc(self.sem[eng], 1)

    def number(self):
        for ops in self.q.values():
            n = 0
            for op in ops:
                if op.used:
                    n += 1
                    op.val = n


class Banks:

    def __init__(self, tiles):
        self.tiles, self.free, self.n, self.held = tiles, [None] * len(tiles), 0, set()

    def get(self, hold=False):
        while self.n % len(self.tiles) in self.held:
            self.n += 1
        i = self.n % len(self.tiles)
        self.n += 1
        if hold:
            self.held.add(i)
        return i, self.tiles[i], self.free[i]

    def done(self, i, *ops):
        self.free[i] = list(ops)
        self.held.discard(i)


def build(nc, x, cols, tab, w, lo2, out, stop=None, dbg=None):
    ctx = ExitStack()
    with ctx:
        Q = Queues(nc, ctx)
        at = [16512]

        def place(name, shape, dt, off=None):
            size = 4 * int(np.prod(shape[1:]))
            if off is None:
                off = at[0]
                at[0] += (size + 31) // 32 * 32
            return nc.alloc_sbuf_tensor_at(name, shape, dt, offset=off)

        X = place("X", [P, KT, T], F32)
        hh_at = at[0]
        HH = place("HH", [P, KT, T], F32R)
        HL = place("HL", [P, KT, T], F32R)
        w_at = at[0]
        st_at = at[0]
        ST = place("ST", [P, 3, 2048], F32)
        WH = place("WH", [P, 3, 2048], F32R)
        WL = place("WL", [P, 3, 2048], F32R)
        ar_at = at[0]
        at[0] += 67648
        GH = place("GH", [P, 16, T], F32R, ar_at)
        GL = place("GL", [P, 16, T], F32R, ar_at + 32768)
        CC = place("CC", [P, NCOL], F32)
        TB = place("TB", [P, NMAIN], F32)
        MOD = place("MOD", [P, 96], F32)
        ADA = place("ADA", [P, 2, 512], F32)
        EX = place("EX", [P, 512], F32)
        RST = place("RST", [P, T], F32)
        ACC = place("ACC", [P, T], F32)
        TMP = place("TMP", [P, 2, T], F32)
        SM = place("SM", [P, 64], F32)
        assert at[0] <= 229368, at[0]

        def col(name, i=0):
            a, n = COLS[name]
            assert i < n
            return CC[:, a + i:a + i + 1]

        EPS = {1e-6: 0, 64e-5: 1}

        def eps_col(v):
            a, _ = TAB["eps"]
            return TB[:, a + EPS[v]:a + EPS[v] + 1]

        def tb(name, rows=slice(0, P)):
            a, n = TAB[name]
            return TB[rows, a:a + n]

        PS = [ctx.enter_context(nc.psum_tensor(f"ps{i}", [P, 512], F32)) for i in range(8)]
        big = Banks(PS[0:4])
        sml = Banks(PS[4:8])

        sem = {}

        def semaphore(name):
            sem[name] = ctx.enter_context(nc.semaphore(name))
            return sem[name]

        s_x, s_cols, s_tab = semaphore("s_x"), semaphore("s_cols"), semaphore("s_tab")
        s_st = [semaphore(f"s_st{i}") for i in range(3)]
        s_ad = [semaphore(f"s_ad{i}") for i in range(8)]
        s_lo = semaphore("s_lo")
        s_out = semaphore("s_out")

        sched = order()

        class Weights:

            def __init__(self):
                self.loads, self.entries = 0, 0
                self.landed, self.read, self.split, self.used = {}, {}, {}, {}
                self.chunk, self.where = [], []
                for pos, (name, _) in enumerate(sched):
                    self.where.append(len(self.chunk))
                    if name != "ada":
                        self.chunk.append(pos)
                self.limit, self.fence = len(sched), []
                self.turns = [0, 0, 0]
                self.due, self.gentle = [], False

            def shape(self, j):
                name, i = sched[self.chunk[j]]
                return STREAM[name]

            def load(self):
                pos = self.loads
                self.loads += 1
                s = pos % 3
                name, i = sched[pos]
                n, kt, c = STREAM[name]
                src = w[name][i]
                self.landed[pos] = Q.dma("sp", ST[:, s, 0:kt * c], src, s_st[s], self.turns[s],
                                         self.read.get(pos - 3), self.fence)
                self.turns[s] += 1

            def entry(self):
                pos = self.entries
                while self.loads <= pos:
                    self.load()
                self.entries += 1
                s = pos % 3
                name, i = sched[pos]
                _, kt, c = STREAM[name]
                n = kt * c
                if name == "ada":
                    self.read[pos] = A.sums(i, ST[:, s, 0:n].rearrange("p (k c) -> p k c", k=kt),
                                            self.landed[pos])
                else:
                    j = self.where[pos]
                    d = j % 3
                    hi = Q.act(lambda e: e.activation(WH[:, d, 0:n], ST[:, s, 0:n], ACT.Copy),
                               self.landed[pos], self.used.get(j - 3), self.fence)
                    done = self.split[j] = self.read[pos] = [hi]
                    parts = 4 if self.gentle else 1
                    for q in range(parts):
                        c = slice(n * q // parts, n * (q + 1) // parts)
                        self.due.append(lambda c=c: done.append(Q.dve(lambda e: e.tensor_tensor(
                            WL[:, d, c], ST[:, s, c], WH[:, d, c].bitcast(F32), ALU.subtract), hi)))
                    if not self.gentle:
                        self.settle(parts)
                while self.loads < pos + (3 if self.gentle else 4) and self.loads < min(len(sched), self.limit):
                    self.load()

            def settle(self, n=4):
                while n and self.due:
                    self.due.pop(0)()
                    n -= 1

            def cut(self, j):
                while j not in self.split and self.entries < min(len(sched), self.limit):
                    self.settle()
                    self.entry()

            def take(self, j):
                A.reduce()
                self.settle()
                self.cut(j + 2)
                s = j % 3
                _, kt, c = self.shape(j)

                def view(W):
                    return W[:, s, 0:kt * c].rearrange("p (k c) -> p k c", k=kt)
                return view(WH), view(WL), self.split[j]

        W = Weights()
        turn = [0]
        h_free = [None]

        def next_chunk():
            turn[0] += 1
            return turn[0] - 1

        d_cols = Q.dma("sp", CC[:, :], cols, s_cols, 0)
        d_x = Q.dma("act", X[:, :, :], x, s_x, 0)
        d_tab = Q.dma("act", TB[:, :], tab[:, 0:NMAIN], s_tab, 0)

        o_cs = Q.act(lambda e: e.activation(SM[:, 0:8], CC[:, 0:8], ACT.Silu), d_cols)

        class Ada:

            def __init__(self):
                self.pending, self.cols = [], {}
                self.acc, self.used = [None, None], [None, None]

            def sums(self, n, tile, landed):
                b, half = n // 2, n % 2
                d = b % 2
                for q in range(4):
                    cc = SM[:, 4 * half + q:4 * half + q + 1]
                    if half == 0 and q == 0:
                        o = Q.dve(lambda e, cc=cc: e.tensor_scalar(ADA[:, d, :], tile[:, 0, :], cc, None,
                                                                   ALU.mult), landed, o_cs, self.used[d])
                    else:
                        o = Q.dve(lambda e, cc=cc, q=q: e.scalar_tensor_tensor(
                            out=ADA[:, d, :], in0=tile[:, q, :], scalar=cc, in1=ADA[:, d, :], op0=ALU.mult,
                            op1=ALU.add), landed, self.acc[d])
                    self.acc[d] = o
                if half:
                    self.pending.append((b, ADA[:, d, :], o, d))
                return [o]

            def columns(self, b, acc, ready):
                i, ps, free = sml.get()
                for j in range(4):
                    m = Q.pe(lambda e, j=j, ps=ps: e.matmul(ps[:, j:j + 1], acc[:, 128 * j:128 * j + 128],
                                                     tb("ones")[:, 0:1], start=True, stop=True),
                             ready, free, d_tab)
                a = COLS["ada_b"][0] + 4 * b
                o = Q.dve(lambda e, ps=ps: e.tensor_tensor(MOD[:, 4 * b:4 * b + 4], ps[:, 0:4], CC[:, a:a + 4],
                                                    ALU.add), m)
                sml.done(i, o)
                for j in range(4):
                    self.cols[4 * b + j] = o
                return m

            def reduce(self):
                for b, acc, ready, d in self.pending:
                    self.used[d] = self.columns(b, acc, ready)
                self.pending = []

            def need(self, layer, which):
                last = 48 * layer + 8 * which + 7
                while last not in self.cols:
                    self.reduce()
                    if last not in self.cols:
                        W.entry()
                return self.cols[last]

            def begin(self):
                W0 = place("W0", [P, 8, 2048], F32, ar_at)
                S0 = place("S0", [P, 2048], F32, hh_at)
                o = None
                for k in range(8):
                    src = w["ada"].rearrange("(b h) p f -> b h p f", h=2)[0:4, k // 4, :,
                                                                          512 * (k % 4):512 * (k % 4) + 512]
                    d = Q.dma("sp" if k % 2 else "act", W0[:, k, :].rearrange("p (b f) -> p b f", b=4),
                              src.rearrange("b p f -> p b f"), s_ad[k], 0)
                    cc = SM[:, k:k + 1]
                    if k == 0:
                        o = Q.dve(lambda e, k=k, cc=cc: e.tensor_scalar(S0[:, :], W0[:, k, :], cc, None,
                                                                        ALU.mult), d, o_cs)
                    else:
                        o = Q.dve(lambda e, k=k, cc=cc: e.scalar_tensor_tensor(
                            out=S0[:, :], in0=W0[:, k, :], scalar=cc, in1=S0[:, :], op0=ALU.mult,
                            op1=ALU.add), d, o)
                for b in (2, 3, 0, 1):
                    m = self.columns(b, S0[:, 512 * b:512 * b + 512], o)
                h_free[0] = [m, o]

        A = Ada()

        def modcol(layer, which, k):
            a = 48 * layer + 8 * which + k
            return MOD[:, a:a + 1]

        tmp_free = [None, None]
        tmp_n = [0]

        def tmp():
            i = tmp_n[0] % 2
            tmp_n[0] += 1
            return i, TMP[:, i, :], tmp_free[i]

        rms_state = {"acc": None, "acc_free": None, "rst_free": None}

        def square_add(k, ready):
            i, t, free = tmp()
            if k == 0:
                o = Q.act(lambda e: e.activation(ACC[:, :], X[:, k, :], ACT.Square), ready,
                          rms_state["acc_free"])
                rms_state["acc"] = o
                return
            o = Q.act(lambda e: e.activation(t, X[:, k, :], ACT.Square), ready, free)
            o = Q.pool(lambda e: e.tensor_tensor(ACC[:, :], ACC[:, :], t, ALU.add), o, rms_state["acc"])
            tmp_free[i] = o
            rms_state["acc"] = o

        def rsqrt(dst, t, ps, o, scale, eps, *free):
            Q.table("natural_log_exp_and_others")
            n = dst.shape[0]
            a = Q.act(lambda e, ps=ps: e.activation(dst, ps, ACT.Ln, scale=scale, bias=eps_col(eps)[0:n]), o, free)
            a = Q.act(lambda e: e.activation(dst, dst, ACT.Exp, scale=-0.5), a)
            b = Q.act(lambda e: e.activation(t, dst, ACT.Square), a)
            r = Q.dve(lambda e, ps=ps: e.scalar_tensor_tensor(out=t, in0=ps, scalar=eps / scale, in1=t, op0=ALU.add,
                                                       op1=ALU.mult), b)
            b = Q.dve(lambda e: e.tensor_scalar(t, t, -0.5 * scale, 1.5, ALU.mult, ALU.add), r)
            return r, Q.dve(lambda e: e.tensor_tensor(dst, dst, t, ALU.mult), b)

        def rsqrt_parts(dst, t, ps, o, scale, eps, *free):
            Q.table("natural_log_exp_and_others")
            n = dst.shape[0]
            a = Q.act(lambda e, ps=ps: e.activation(dst, ps, ACT.Ln, scale=scale, bias=eps_col(eps)[0:n]), o, free)
            a = Q.act(lambda e: e.activation(dst, dst, ACT.Exp, scale=-0.5), a)
            b = Q.act(lambda e: e.activation(t, dst, ACT.Square), a)

            def rest():
                r = Q.dve(lambda e, ps=ps: e.scalar_tensor_tensor(out=t, in0=ps, scalar=eps / scale, in1=t,
                                                           op0=ALU.add, op1=ALU.mult), b)
                c = Q.dve(lambda e: e.tensor_scalar(t, t, -0.5 * scale, 1.5, ALU.mult, ALU.add), r)
                return r, Q.dve(lambda e: e.tensor_tensor(dst, dst, t, ALU.mult), c)
            return rest

        def rms():
            i, ps, free = sml.get()
            m = Q.pe(lambda e, ps=ps: e.matmul(ps[:, :], tb("ones"), ACC[:, :], start=True, stop=True),
                     rms_state["acc"], free, d_tab)
            rms_state["acc_free"] = m
            n, t, tf = tmp()
            r, o = rsqrt(RST[:, :], t, ps[:, :], m, 1.0 / D, 1e-6, rms_state["rst_free"], tf)
            sml.done(i, r)
            tmp_free[n] = o
            return o

        def split_into(H, L, src, ready, free, bias=0.0):
            h = Q.act(lambda e: e.activation(H, src, ACT.Identity, bias=bias), ready, free)
            if isinstance(bias, float):
                lo = Q.dve(lambda e: e.tensor_tensor(L, src, H.bitcast(F32), ALU.subtract), h)
            else:
                lo = Q.dve(lambda e: e.scalar_tensor_tensor(out=L, in0=src, scalar=bias, in1=H.bitcast(F32),
                                                            op0=ALU.add, op1=ALU.subtract), h)
            return [h, lo]

        def split_late(H, L, src, ready, free, bias=0.0):
            both = [Q.act(lambda e: e.activation(H, src, ACT.Identity, bias=bias), ready, free)]

            def rest():
                hi = both[0]
                if isinstance(bias, float):
                    both.append(Q.dve(lambda e: e.tensor_tensor(L, src, H.bitcast(F32), ALU.subtract), hi))
                else:
                    both.append(Q.dve(lambda e: e.scalar_tensor_tensor(
                        out=L, in0=src, scalar=bias, in1=H.bitcast(F32), op0=ALU.add, op1=ALU.subtract), hi))
            return both, rest

        gain = {}

        def mod_gain(name, gname, g0, layer, which):
            o = A.need(layer, which)
            s = 8 + 8 * (len(gain) % 4)
            a = 48 * layer + 8 * which
            g = COLS[gname][0] + g0
            o = Q.dve(lambda e: e.scalar_tensor_tensor(out=SM[:, s:s + 8], in0=MOD[:, a:a + 8], scalar=1.0,
                                                       in1=CC[:, g:g + 8], op0=ALU.add, op1=ALU.mult),
                      o, d_cols)
            gain[name] = s
            return lambda k: SM[:, s + k:s + k + 1], o

        def norm_split(gcol, gready, bcol, rstd):
            ready = []
            for k in range(KT):
                i, t, free = tmp()
                o = Q.dve(lambda e, k=k, t=t: e.scalar_tensor_tensor(
                    out=t, in0=X[:, k, :], scalar=gcol(k), in1=RST[:, :], op0=ALU.mult, op1=ALU.mult),
                    rstd, gready, free)
                b = bcol(k) if bcol else 0.0
                r, rest = split_late(HH[:, k, :], HL[:, k, :], t, o, h_free[0], b)
                if k:
                    late()
                late = rest
                tmp_free[i] = r
                ready.append(r)
            late()
            rms_state["rst_free"] = o
            return ready

        def dense(nchunk, H, L, ready, consume):
            m = 0
            for n in range(nchunk):
                j = next_chunk()
                wh, wl, cut = W.take(j)
                _, kt, c = W.shape(j)
                cols_ = list(range(0, c, P))
                for group in ([cols_] if n == 0 else [[c0] for c0 in cols_]):
                    got, last = [big.get() for _ in group], [None] * len(group)
                    for k in range(kt):
                        for g_, c0 in enumerate(group):
                            _, ps, free = got[g_]
                            for part, (a, b) in enumerate(((wh, H), (wh, L), (wl, H))):
                                last[g_] = o = Q.pe(lambda e, ps=ps, a=a, b=b, k=k, c0=c0, part=part, kt=kt:
                                                    e.matmul(ps[:, :], a[:, k, c0:c0 + P], b[:, k, :],
                                                             start=(k == 0 and part == 0),
                                                             stop=(k == kt - 1 and part == 2)),
                                                    free, cut, ready[k])
                    for g_ in range(len(group)):
                        i, ps, _ = got[g_]
                        big.done(i, *consume(m, ps, last[g_]))
                        m += 1
                W.used[j] = o
            return o

        def residual(gcol, gready, squares):
            def consume(m, ps, o):
                if gcol is None:
                    r = Q.dve(lambda e, ps=ps: e.tensor_tensor(X[:, m, :], X[:, m, :], ps[:, :], ALU.add), o)
                else:
                    r = Q.dve(lambda e, ps=ps: e.scalar_tensor_tensor(out=X[:, m, :], in0=ps[:, :], scalar=gcol(m),
                                                               in1=X[:, m, :], op0=ALU.mult, op1=ALU.add),
                              o, gready)
                x_ready[m] = r
                if squares:
                    square_add(m, r)
                return [r]
            return consume

        x_ready = [d_x] * KT

        def finish():
            o = x_ready
            Q.dma("sp", out, X[:, :, :], s_out, 0, o)

        g_free = [None] * 16

        def mlp(layer):
            gc, gr = mod_gain(f"mlp{layer}", "norm_g", 16 * layer + 8, layer, 4)
            br = A.need(layer, 3)
            ready = norm_split(gc, [gr, br], lambda k: modcol(layer, 3, k), rms())
            gt = A.need(layer, 5)
            for g in range(2):
                gready = [None] * 16

                def hidden(m, ps, o):
                    i, t, free = tmp()
                    r = Q.act(lambda e, ps=ps: e.activation(t, ps[:, :], ACT.Relu), o, free)
                    s = Q.act(lambda e: e.activation(t, t, ACT.Square), r)
                    h = split_into(GH[:, m, :], GL[:, m, :], t, s, g_free[m])
                    tmp_free[i] = h
                    gready[m] = h
                    return [r]

                h_free[0] = dense(8, HH, HL, ready, hidden)
                last = dense(8, GH, GL, gready, residual(lambda m: modcol(layer, 5, m), gt, g == 1))
                for m in range(16):
                    g_free[m] = last

        def conv_mixer():
            for k in range(KT):
                square_add(k, d_x)
            rstd = rms()
            W.limit = 1
            W.cut(0)
            A.begin()
            W.limit = len(sched)
            gc, gr = mod_gain("conv", "norm_g", 0, 0, 1)
            br = A.need(0, 0)
            ready = norm_split(gc, [gr, br], lambda k: modcol(0, 0, k), rstd)
            U = place("U", [P, 2, T + 2], F32, ar_at + 32768 + 16384)
            CV = place("CV", [P, 2, T], F32, ar_at + 32768 + 16384 + 8192)
            begun = h_free[0]
            z = Q.pool(lambda e: e.memset(U[:, :, 0:2], 0.0), begun)
            u_free, cv, yready = [None, None], [None, None], [None] * KT
            cs = {}

            def consume(m, ps, o):
                grp, r = m // 6, m % 6
                if r in (0, 2):
                    f = r // 2
                    i, t, free = tmp()
                    c = Q.act(lambda e, ps=ps: e.activation(t, ps[:, :], ACT.Copy), o, free)
                    cs[f] = (i, t, c)
                    return [c]
                if r in (1, 3):
                    f = r // 2
                    k = 2 * grp + f
                    i, t, c = cs[f]
                    u = Q.dve(lambda e, ps=ps: e.tensor_tensor(U[:, f, 2:T + 2], ps[:, :], t, ALU.mult), o, c, z,
                              u_free[f])
                    tmp_free[i] = u
                    a = Q.dve(lambda e: e.tensor_scalar(CV[:, f, :], U[:, f, 0:T], col("conv_w", k), None,
                                                        ALU.mult), u, cv[f])
                    for j in (1, 2):
                        a = Q.dve(lambda e, j=j: e.scalar_tensor_tensor(
                            out=CV[:, f, :], in0=U[:, f, j:j + T], scalar=col("conv_w", 8 * j + k),
                            in1=CV[:, f, :], op0=ALU.mult, op1=ALU.add), a)
                    u_free[f] = a
                    cv[f] = a
                    return [u]
                f = r - 4
                k = 2 * grp + f
                y = Q.dve(lambda e, ps=ps: e.tensor_tensor(CV[:, f, :], CV[:, f, :], ps[:, :], ALU.mult), o, cv[f])
                h = split_into(GH[:, k, :], GL[:, k, :], CV[:, f, :], y, begun)
                cv[f] = h
                yready[k] = h
                return [y]

            h_free[0] = dense(12, HH, HL, ready, consume)
            gt = A.need(0, 2)
            last = dense(4, GH, GL, yready, residual(lambda m: modcol(0, 2, m), gt, True))
            for m in range(16):
                g_free[m] = [last] + Q.last("dve", "act")

        def inverse(lt, tt, t, u, tb2, levels, banks, ready):
            n_mat = lt.shape[1]
            halves = [range(a, min(a + 4, n_mat)) for a in range(0, n_mat, 4)]
            tt_o, t_o, u_free = {}, {}, {}
            for h, r in enumerate(halves):
                i, ps, free = banks.get()
                for n in r:
                    c = P * (n - r[0])
                    o = Q.pe(lambda e, n=n, c=c, ps=ps: e.transpose(ps[:, c:c + P], tt[:, n, :], tb("ident")),
                             ready, free)
                w_ = P * len(r)
                o = Q.act(lambda e, r=r, ps=ps, w_=w_: e.activation(
                    t[:, r[0]:r[-1] + 1, :], ps[:, 0:w_].rearrange("p (n c) -> p n c", c=P), ACT.Copy), o)
                banks.done(i, o)
                t_o[h], tt_o[h] = [o], [ready]
            yield
            for lev in range(1, levels):
                mask = tb2(f"low{lev}")
                for h, r in enumerate(halves):
                    a, b = r[0], r[-1] + 1
                    k = len(r)
                    i, ps, free = banks.get()
                    for n in r:
                        c = P * (n - a)
                        o = Q.pe(lambda e, n=n, c=c, ps=ps: e.matmul(ps[:, c:c + P], lt[:, n, :], t[:, n, :],
                                                                     start=True, stop=True),
                                 t_o[h], free)
                    mb = mask[:, None, :].broadcast_to((P, k, P))
                    uo = Q.dve(lambda e, a=a, b=b, ps=ps, mb=mb, k=k: e.tensor_tensor(
                        u[:, a:b, :], ps[:, 0:P * k].rearrange("p (n c) -> p n c", c=P), mb, ALU.mult),
                        o, u_free.get(h))
                    banks.done(i, uo)
                    u_free[h] = uo
                    yield
                for h, r in enumerate(halves):
                    a, b = r[0], r[-1] + 1
                    k = len(r)
                    more = lev < levels - 1
                    if more:
                        i, ps, free = banks.get()
                        for n in r:
                            c = P * (n - a)
                            o1 = Q.pe(lambda e, n=n, c=c, ps=ps: e.matmul(
                                ps[:, c:c + P], tt[:, n, :], u[:, n, :], start=True, stop=True),
                                u_free[h], tt_o[h], free)
                        o = Q.dve(lambda e, a=a, b=b, ps=ps, k=k: e.tensor_tensor(
                            t[:, a:b, :], t[:, a:b, :], ps[:, 0:P * k].rearrange("p (n c) -> p n c", c=P),
                            ALU.add), o1)
                        banks.done(i, o)
                        t_o[h] = [o]
                    i, ps, free = banks.get()
                    for n in r:
                        c = P * (n - a)
                        o2 = Q.pe(lambda e, n=n, c=c, ps=ps: e.matmul(
                            ps[:, c:c + P], u[:, n, :], tt[:, n, :], start=True, stop=True),
                            u_free[h], tt_o[h], free)
                    o = Q.dve(lambda e, a=a, b=b, ps=ps, k=k: e.tensor_tensor(
                        tt[:, a:b, :], tt[:, a:b, :], ps[:, 0:P * k].rearrange("p (n c) -> p n c", c=P),
                        ALU.add), o2)
                    banks.done(i, o)
                    tt_o[h] = [o]
                    u_free[h] = [o2]
                    yield
            yield [o for v in tt_o.values() for o in v]

        def interleave(*gens):
            gens = list(gens)
            while gens:
                gens = [g for g in gens if next(g, gens) is not gens]

        def rwkv_mixer():
            NE = float(np.exp(-0.5))
            A.need(1, 5)
            GBT = EX
            rstd = rms()
            gc, gr = mod_gain("rwkv", "norm_g", 16, 1, 1)
            HT = place("HT", [P, KT, T + 1], F32, ar_at)
            base = ar_at + 16448
            RR = place("RR", [P, KT, T], F32, base)
            KK = place("KK", [P, KT, T], F32, base + 16384)
            VV = place("VV", [P, KT, T], F32, base + 32768)
            XX = place("XX", [P, 512], F32, base + 49152)
            fence = Q.last("pe", "act", "dve", "pool")
            z = Q.pool(lambda e: e.memset(HT[:, :, 0:1], 0.0), fence)
            ht = []
            for k in range(KT):
                i, t, free = tmp()
                o = Q.dve(lambda e, k=k, t=t: e.scalar_tensor_tensor(
                    out=t, in0=X[:, k, :], scalar=gc(k), in1=RST[:, :], op0=ALU.mult, op1=ALU.mult),
                    rstd, gr, free)
                o = Q.act(lambda e, k=k, t=t: e.activation(HT[:, k, 1:T + 1], t, ACT.Identity,
                                                           bias=modcol(1, 0, k)), o, fence)
                tmp_free[i] = o
                ht.append(o)
            diff = [Q.pool(lambda e, k=k: e.tensor_tensor(VV[:, k, :], HT[:, k, 0:T], HT[:, k, 1:T + 1],
                                                          ALU.subtract), z, ht[k]) for k in range(KT)]

            def mix(n):
                ready = []
                for k in range(KT):
                    i, t, free = tmp()
                    o = Q.dve(lambda e, k=k, t=t: e.scalar_tensor_tensor(
                        out=t, in0=VV[:, k, :], scalar=col("mu", 8 * n + k), in1=HT[:, k, 1:T + 1],
                        op0=ALU.mult, op1=ALU.add), diff[k], free)
                    r, rest = split_late(HH[:, k, :], HL[:, k, :], t, o, h_free[0])
                    if k:
                        late()
                    late = rest
                    tmp_free[i] = r
                    ready.append(r)
                late()
                return ready

            def lora(j, jobs, ready):
                wh, wl, cut = W.take(j)
                for c0, r0, fn, dst in jobs:
                    i, ps, free = big.get()
                    for k in range(KT):
                        for part, (a, b) in enumerate(((wh, HH), (wh, HL), (wl, HH))):
                            o = Q.pe(lambda e, a=a, b=b, k=k, c0=c0, part=part, ps=ps: e.matmul(
                                ps[:, :], a[:, k, c0:c0 + P], b[:, k, :], start=(k == 0 and part == 0),
                                stop=(k == KT - 1 and part == 2)), free, cut, ready[k])
                    r1 = P if r0 != 0 or dst is not WA else 64
                    r = Q.act(lambda e, r0=r0, r1=r1, ps=ps, fn=fn, dst=dst: e.activation(
                        dst[r0:r1, :], ps[r0:r1, :], fn), o)
                    big.done(i, r)
                W.used[j] = o
                h_free[0] = o
                return r

            WA, GA, GB = ADA[:, 0, :], ADA[:, 1, :], GBT[:, :]
            j = next_chunk()
            lora(j, [(0, 0, ACT.Tanh, WA)], mix(1))
            wa = lora(j, [(0, 64, ACT.Copy, WA)], mix(4))
            ga = lora(next_chunk(), [(0, 0, ACT.Sigmoid, GA), (32, 96, ACT.Sigmoid, GB)], mix(5))
            W.limit = sched.index(("wo", 0))
            for dst, n in ((RR, 0), (KK, 2), (VV, 3)):
                def keep(m, ps, o, dst=dst):
                    return [Q.act(lambda e, ps=ps: e.activation(dst[:, m, :], ps[:, :], ACT.Copy), o)]
                h_free[0] = dense(4, HH, HL, mix(n), keep)

            fence = Q.last("pe", "act", "dve", "pool")
            at_ = [w_at]

            def scratch(name, shape):
                a = at_[0]
                at_[0] += 4 * int(np.prod(shape[1:]))
                return place(name, shape, F32, a)

            LO2 = scratch("LO2", [P, 3, D])
            TB2 = scratch("TB2", [P, 8, P])
            BK = scratch("BK", [P, 8, P])
            AR = scratch("AR", [P, 2, 8, P])
            GT = scratch("GT", [P, 2, 2, 8, P])
            BT = scratch("BT", [P, 2, 2, 8, 64])
            VS = scratch("VS", [P, 2, 2, 8, 64])
            LT = scratch("LT", [P, 8, P])
            TN = scratch("TN", [P, 8, P])
            UN = scratch("UN", [P, 8, P])
            assert at_[0] <= ar_at
            TT = place("TT", [P, 2, 8, P], F32, ar_at)
            TE = place("TE", [P, 4, T], F32, ar_at + 8192)
            SS = XX[:, 0:128]
            SE = XX[:, 128:256]
            X1 = XX[:, 256:320]
            EC = XX[:, 320:336].rearrange("p (b c) -> p b c", b=2)
            d_lo = Q.dma("sp", LO2[:, :, :], lo2, s_lo, 0, fence)
            d_tb = Q.dma("sp", TB2[:, :, :], tab[:, NMAIN:NTAB].rearrange("p (n c) -> p n c", c=P), s_lo, 1,
                         fence)
            d_lo = d_tb

            def tb2(name):
                return TB2[:, (TAB[name][0] - NMAIN) // P, :]

            zx = Q.pool(lambda e: e.memset(XX[:, :], 0.0), fence)
            T1, T2, T3, T5, T6, T0 = TE[:, 0, :], TE[:, 1, :], TE[:, 2, :], TE[:, 3, :], RST[:, :], ACC[:, :]
            F1, F2 = TMP[:, 0, :], TMP[:, 1, :]
            prep_b, inv_b = Banks(PS[0:4]), Banks(PS[4:6])
            PY, PC = PS[6], PS[7]
            state = {}
            first = [fence]
            tprev = {"bk": None, "lt": None, "elem": fence}
            hready = [None] * KT

            def h64(ap):
                return ap.rearrange("p (c t) -> p c t", t=64)

            def prep(m):
                b = m % 2
                st = state[m] = {}
                ms = slice(m * P, m * P + P)
                el = tprev["elem"]
                i, ps, free = prep_b.get()
                o = Q.pe(lambda e, ps=ps: e.matmul(ps[:, :], LO2[0:64, 0, ms], WA[0:64, :], start=True, stop=True),
                         d_lo, free, fence, wa)
                sg = Q.act(lambda e, ps=ps: e.activation(T0, ps[:, :], ACT.Sigmoid, bias=col("w0", m)), o, el)
                prep_b.done(i, sg)
                i, ps, free = prep_b.get()
                o = Q.pe(lambda e, ps=ps: e.matmul(ps[:, :], LO2[64:128, 0, ms], WA[64:128, :], start=True,
                                            stop=True), d_lo, free)
                ao = Q.act(lambda e, ps=ps: e.activation(T5, ps[:, :], ACT.Sigmoid, bias=col("a0", m)), o, el)
                prep_b.done(i, ao)
                kko = Q.dve(lambda e: e.tensor_scalar(T6, KK[:, m, :], col("k_k", m), None, ALU.mult), el)
                yield
                for c in range(8):
                    cs = slice(64 * c, 64 * c + 64)
                    so = Q.dve(lambda e, cs=cs: e.tensor_tensor_scan(T1[:, cs], tb("ones")[:, 0:64], T0[:, cs],
                                                                     0.0, ALU.mult, ALU.add), sg, el)
                yield
                cp = Q.dve(lambda e: e.tensor_tensor(T0, T1, T0, ALU.subtract), so)
                ep = Q.act(lambda e: e.activation(T2, T1, ACT.Exp, scale=-NE), so)
                em = Q.act(lambda e: e.activation(T3, T1, ACT.Exp, scale=NE), so)
                e0 = Q.act(lambda e: e.activation(T0, T0, ACT.Exp, scale=-NE), cp)
                sq = Q.act(lambda e: e.activation(T1, T6, ACT.Square), kko, cp, em)
                yield
                i, ps, free = prep_b.get()
                o = Q.pe(lambda e, ps=ps: e.matmul(ps[:, :], tb("bones"), T1, start=True, stop=True), sq, free)
                nr = Q.dve(lambda e, ps=ps: e.tensor_scalar(F1, ps[:, :], 1e-24, None, ALU.max), o, sfree["f"])
                prep_b.done(i, nr)
                a_ = Q.act(lambda e: e.activation(T1, F1, ACT.Ln), nr, o)
                a_ = Q.act(lambda e: e.activation(T1, T1, ACT.Exp, scale=-0.5), a_)
                a_ = Q.act(lambda e: e.activation(F2, T1, ACT.Square), a_)
                yield
                o = Q.dve(lambda e: e.scalar_tensor_tensor(out=F2, in0=F1, scalar=-0.5, in1=F2, op0=ALU.mult,
                                                           op1=ALU.mult), a_)
                o = Q.dve(lambda e: e.scalar_tensor_tensor(out=T1, in0=F2, scalar=1.5, in1=T1, op0=ALU.add,
                                                           op1=ALU.mult), o)
                sfree["f"] = o
                yield
                kn = Q.dve(lambda e: e.tensor_tensor(T6, T6, T1, ALU.mult), o)
                o = Q.dve(lambda e: e.tensor_scalar(T1, T5, 1.0, col("k_a", m), ALU.subtract, ALU.mult), ao,
                          kn)
                k2 = Q.dve(lambda e: e.scalar_tensor_tensor(out=KK[:, m, :], in0=T1, scalar=1.0,
                                                            in1=KK[:, m, :], op0=ALU.add, op1=ALU.mult), o)
                yield "elements"
                old = state.get(m - 2, {}).get("done")
                aa = Q.dve(lambda e: e.scalar_tensor_tensor(out=AR[:, b, :, 0:64], in0=h64(T6), scalar=-1.0,
                                                            in1=h64(T0), op0=ALU.mult, op1=ALU.mult),
                           kn, e0, old)
                rr = Q.dve(lambda e: e.tensor_tensor(AR[:, b, :, 64:128], h64(RR[:, m, :]), h64(T2),
                                                     ALU.mult), ep, old)
                ec = Q.act(lambda e: e.activation(EC[:, b, :], h64(T2)[:, :, 63], ACT.Copy), ep, old, zx)
                yield
                o = Q.dve(lambda e: e.tensor_tensor(T5, T5, T6, ALU.mult), aa)
                for hh in range(2):
                    rows = slice(64 * hh, 64 * hh + 64)
                    ba, ka = (0, 64) if hh == 0 else (64, 0)
                    b1 = Q.dve(lambda e, rows=rows, ba=ba: e.tensor_tensor(
                        BK[rows, :, ba:ba + 64], h64(T5[rows]), h64(T3[rows]), ALU.mult), o, em, tprev["bk"])
                    b2 = Q.dve(lambda e, rows=rows, ka=ka: e.tensor_tensor(
                        BK[rows, :, ka:ka + 64], h64(KK[rows, m, :]), h64(T3[rows]), ALU.mult), k2)
                    yield
                rk = Q.dve(lambda e: e.scalar_tensor_tensor(out=T1, in0=RR[:, m, :], scalar=col("r_k", m),
                                                            in1=KK[:, m, :], op0=ALU.mult, op1=ALU.mult), k2)
                tprev["elem"] = [rk, b2, ec]
                gts = {}
                for half in range(2):
                    for hh in range(2):
                        rows = slice(64 * hh, 64 * hh + 64)
                        i, ps, free = prep_b.get()
                        for q in range(4):
                            c = 4 * half + q
                            o = Q.pe(lambda e, c=c, q=q, rows=rows, ps=ps: e.matmul(
                                ps[:, P * q:P * q + P], BK[rows, c, :], AR[rows, b, c, :], start=True,
                                stop=True), b1, b2, aa, rr, free)
                        mk = tb("rwm")[:, None, :].broadcast_to((P, 4, P))
                        g = Q.dve(lambda e, half=half, hh=hh, ps=ps, mk=mk: e.tensor_tensor(
                            GT[:, b, hh, 4 * half:4 * half + 4, :],
                            ps[:, :].rearrange("p (n c) -> p n c", c=P), mk, ALU.mult), o, old)
                        prep_b.done(i, g)
                        gts[hh] = g
                        yield
                i, ps, free = prep_b.get()
                bo = Q.pe(lambda e, ps=ps: e.matmul(ps[:, :], tb("bones"), T1, start=True, stop=True), rk, free)
                tprev["elem"] = [rk, b2, ec, bo]
                bonus = Q.dve(lambda e, ps=ps: e.tensor_tensor(RR[:, m, :], ps[:, :], VV[:, m, :], ALU.mult), bo, rr)
                prep_b.done(i, bonus)
                vz = Q.pool(lambda e: e.memset(VS[:, b, :, :, :], 0.0), old, fence)
                l0 = Q.dve(lambda e: e.tensor_tensor(
                    LT[:, :, :].rearrange("p c (h t) -> p h c t", h=2), GT[:, b, :, :, 0:64],
                    tb("bones").rearrange("p (h t) -> p h t", h=2)[:, :, None, :].broadcast_to((P, 2, 8, 64)),
                    ALU.mult), gts[0], gts[1], tprev["lt"])
                mk = tb2("upp0")[:, None, :].broadcast_to((P, 8, P))
                idb = tb("ident")[:, None, :].broadcast_to((P, 8, P))
                t0 = Q.pool(lambda e: e.tensor_tensor(TT[:, b, :, :], LT[:, :, :], mk, ALU.mult), l0, old,
                            d_tb, fence)
                t0 = Q.pool(lambda e: e.tensor_tensor(TT[:, b, :, :], TT[:, b, :, :], idb, ALU.add), t0)
                bt = []
                for hh in range(2):
                    rows = slice(64 * hh, 64 * hh + 64)
                    i, ps, free = prep_b.get()
                    for c in range(8):
                        o = Q.pe(lambda e, c=c, rows=rows, ps=ps: e.transpose(
                            ps[:, 64 * c:64 * c + 64], BK[rows, c, :], tb("idk", rows)), free)
                    t_ = Q.act(lambda e, hh=hh, ps=ps: e.activation(BT[:, b, hh, :, :], h64(ps[:, :]),
                                                                    ACT.Copy), o, old)
                    prep_b.done(i, t_)
                    bt.append(t_)
                    yield
                tprev["bk"] = o
                i, ps, free = prep_b.get()
                for c in range(8):
                    for hh in range(2):
                        o = Q.pe(lambda e, c=c, hh=hh, ps=ps: e.matmul(
                            ps[64 - 64 * hh:128 - 64 * hh, 64 * c:64 * c + 64],
                            VV[:, m, 64 * c:64 * c + 64], tb("ident")[:, 64 * hh:64 * hh + 64],
                            start=True, stop=True), free)
                for hh in range(2):
                    rows = slice(64 - 64 * hh, 128 - 64 * hh)
                    v = Q.act(lambda e, hh=hh, rows=rows, ps=ps: e.activation(
                        VS[rows, b, hh, :, :], h64(ps[rows, :]), ACT.Copy), o, vz)
                    bt.append(v)
                prep_b.done(i, v)
                vdone = [o, bonus]
                yield
                i, ps, free = prep_b.get()
                Q.pe(lambda e, ps=ps: e.matmul(ps[:, :], LO2[:, 1, ms], GA, start=True, stop=False), free, ga)
                o = Q.pe(lambda e, ps=ps: e.matmul(ps[:, :], LO2[96:128, 2, ms], GB[96:128, :], start=False,
                                            stop=True))
                go = Q.act(lambda e, ps=ps: e.activation(VV[:, m, :], ps[:, :], ACT.Copy), o, vdone)
                prep_b.done(i, go)
                tto = None
                yield
                for v in inverse(LT[:, :, :], TT[:, b, :, :], TN[:, :, :], UN[:, :, :], tb2, 6, inv_b,
                                 [t0, tprev["lt"]]):
                    if v:
                        tto = v
                    yield
                tprev["lt"] = Q.last("pe")
                st.update(pre=[aa, rr, gts[0], gts[1]] + bt, tt=tto, ec=ec, bonus=bonus, go=go)

            sfree = {"s": zx, "x1": None, "pc": None, "py": None, "f": Q.last("act", "dve")}

            def chain(m):
                b = m % 2
                st = state[m]
                s = Q.pool(lambda e: e.memset(SS, 0.0), sfree["s"])
                x1, pc = sfree["x1"], sfree["pc"]
                so = [s]
                ry = None
                for c in range(8):
                    for hh in range(2):
                        r = slice(64 * hh, 64 * hh + 64)
                        Q.pe(lambda e, r=r, c=c: e.matmul(PC[r, 0:64], AR[:, b, c, 0:64], SS[:, r],
                                                          start=True, stop=False), so, st["pre"], pc)
                        o = Q.pe(lambda e, r=r, c=c, hh=hh: e.matmul(
                            PC[r, 0:64], GT[:, b, hh, c, 0:64], VS[:, b, hh, c, :], start=False, stop=True))
                    ry = Q.pe(lambda e, c=c: e.matmul(PY[:, 64 * c:64 * c + 64], SS, AR[:, b, c, 64:128],
                                                      start=True, stop=False), sfree["py"])
                    xo = Q.dve(lambda e: e.tensor_copy(X1, PC[:, 0:64]), o, x1)
                    yield
                    o = Q.pe(lambda e, c=c: e.matmul(PC[:, 64:128], TT[:, b, c, :], X1, start=True,
                                                     stop=True), xo, st["tt"], pc)
                    x1 = o
                    v0 = Q.act(lambda e, c=c: e.activation(VS[0:64, b, 0, c, :], PC[0:64, 64:128], ACT.Copy),
                               o)
                    v1 = Q.dve(lambda e, c=c: e.tensor_copy(VS[64:128, b, 1, c, :], PC[64:128, 64:128]), o)
                    yield
                    for hh, vo in ((0, v0), (1, v1)):
                        r = slice(64 * hh, 64 * hh + 64)
                        Q.pe(lambda e, r=r: e.matmul(PC[r, 128:192], tb("ident")[:, r], SS[:, r], start=True,
                                                     stop=False), vo)
                        o = Q.pe(lambda e, r=r, c=c, hh=hh: e.matmul(
                            PC[r, 128:192], BT[:, b, hh, c, :], VS[:, b, hh, c, :], start=False, stop=True),
                            vo)
                    for hh, vo in ((0, v0), (1, v1)):
                        r = slice(64 * hh, 64 * hh + 64)
                        yo = Q.pe(lambda e, r=r, c=c, hh=hh: e.matmul(
                            PY[r, 64 * c:64 * c + 64], VS[:, b, hh, c, :], GT[:, b, hh, c, 64:128],
                            start=False, stop=True))
                    so = []
                    for hh in range(2):
                        r = slice(64 * hh, 64 * hh + 64)
                        so.append(Q.dve(lambda e, r=r, c=c: e.tensor_scalar(
                            SS[r, r], PC[r, 128:192], EC[r, b, c:c + 1], None, ALU.mult), o, st["ec"], ry))
                    pc = so
                    yield
                sfree.update(s=[so, yo], x1=x1, pc=pc)
                st["done"] = [yo, so]
                y = KK[:, m, :]
                yc = Q.act(lambda e: e.activation(y, PY[:, :], ACT.Copy), yo)
                sfree["py"] = yc
                st["y"] = yc

            def tail(m):
                st, y = state[m], KK[:, m, :]
                i, ps, free = prep_b.get()
                yc = st["y"]
                o = Q.pe(lambda e, ps=ps: e.matmul(ps[:, :], tb("bones"), y, start=True, stop=True), yc, free)
                o = Q.dve(lambda e, ps=ps: e.scalar_tensor_tensor(out=y, in0=ps[:, :], scalar=-1.0 / 64, in1=y,
                                                           op0=ALU.mult, op1=ALU.add), o)
                prep_b.done(i, o)
                q = Q.act(lambda e: e.activation(F1, y, ACT.Square), o, sfree["f"])
                yield
                i, ps, free = prep_b.get(hold=True)
                o = Q.pe(lambda e, ps=ps: e.matmul(ps[:, :], tb("bones"), F1, start=True, stop=True), q, free)
                rest = rsqrt_parts(F1, F2, ps[:, :], o, 1.0 / 64, 64e-5)
                yield
                r, o = rest()
                prep_b.done(i, r)
                yield
                o = Q.dve(lambda e: e.scalar_tensor_tensor(out=y, in0=y, scalar=col("ln_w", m), in1=F1,
                                                           op0=ALU.mult, op1=ALU.mult), o)
                o = Q.dve(lambda e: e.scalar_tensor_tensor(out=y, in0=y, scalar=col("ln_b", m),
                                                           in1=RR[:, m, :], op0=ALU.add, op1=ALU.add), o,
                          st["bonus"])
                o = Q.dve(lambda e: e.tensor_tensor(y, y, VV[:, m, :], ALU.mult), o, st["go"])
                hready[m] = split_into(HH[:, m, :], HL[:, m, :], y, o, h_free[0])
                sfree["f"] = o
                yield

            preps = {0: prep(0)}

            def filler(m):
                post = tail(m - 1) if m else iter(())
                cur = preps.get(m + 1, iter(()))
                more = m + 2 < 8
                if more:
                    preps[m + 2] = prep(m + 2)
                for n, _ in enumerate(cur):
                    yield
                    if n % 2 == 1 and n > POST_FROM:
                        if next(post, done) is not done:
                            yield
                        elif more and n > NEXT_FROM:
                            more = next(preps[m + 2]) != "elements"
                            yield
                for _ in post:
                    yield
                while more:
                    more = next(preps[m + 2]) != "elements"
                    yield

            done = object()
            POST_FROM, NEXT_FROM, FILL_STEPS, CHAIN_STEPS = 4, 14, 43, 24
            for _ in preps[0]:
                pass
            preps[1] = prep(1)
            while next(preps[1]) != "elements":
                pass
            for m in range(8):
                fill = filler(m)
                due = 0
                for _ in chain(m):
                    due += FILL_STEPS if m < 7 else 8
                    while due >= CHAIN_STEPS:
                        due -= CHAIN_STEPS
                        next(fill, None)
                for _ in fill:
                    pass
            for _ in tail(7):
                pass
            W.fence = Q.last("pe", "act", "dve", "pool")
            for bk in (big, sml):
                for i in range(4):
                    bk.done(i, *W.fence)
            tmp_free[0] = tmp_free[1] = W.fence
            rms_state["acc_free"] = rms_state["rst_free"] = W.fence
            W.limit = len(sched)
            gt = A.need(1, 2)
            last = dense(4, HH, HL, hready, residual(lambda m: modcol(1, 2, m), gt, True))
            h_free[0] = last
            for m in range(16):
                g_free[m] = Q.last("pe", "dve", "act", "pool")

        def swiglu(layer):
            base = 8 * layer
            ready = norm_split(lambda k: col("ffn_norm", base + k), d_cols, None, rms())
            final = layer == 1
            for g in range(2):
                gready = [None] * 16
                gate = {}

                def hidden(m, ps, o):
                    if m % 2 == 0:
                        i, t, free = tmp()
                        r = Q.act(lambda e, ps=ps: e.activation(t, ps[:, :], ACT.Silu), o, free)
                        gate[0] = (i, t, r)
                        return [r]
                    i, t, r = gate[0]
                    n = m // 2
                    r = Q.dve(lambda e, ps=ps: e.tensor_tensor(t, t, ps[:, :], ALU.mult), r, o)
                    h = split_into(GH[:, n, :], GL[:, n, :], t, r, g_free[n])
                    tmp_free[i] = h
                    gready[n] = h
                    return [r]

                h_free[0] = dense(11, HH, HL, ready, hidden)
                last = dense(8, GH, GL, gready, residual(None, None, g == 1 and not final))
                for m in range(16):
                    g_free[m] = last

        def gdn_mixer():
            rstd = rms()
            for k in range(KT):
                o = Q.dve(lambda e, k=k: e.scalar_tensor_tensor(
                    out=X[:, k, :], in0=X[:, k, :], scalar=col("final_g", k), in1=RST[:, :], op0=ALU.mult,
                    op1=ALU.mult), rstd)
                x_ready[k] = o
                square_add(k, o)
            rms_state["rst_free"] = o
            if stop == "fin":
                return
            ready = norm_split(lambda k: col("attn_norm", k), d_cols, None, rms())
            fence = Q.last("pe", "act", "dve", "pool")
            OF = place("OF", [P, 8, T], F32, ar_at)
            area = [ar_at + 16384]

            def scratch(name, shape):
                size = (4 * int(np.prod(shape[1:])) + 31) // 32 * 32
                area[0] += size
                assert area[0] <= ar_at + 67648, name
                return place(name, shape, F32, area[0] - size)

            TB2 = scratch("TG2", [P, 7, P])
            UU = scratch("UU", [P, 3, T + 3])
            ZZ = [scratch("ZZ0", [P, T])[:, :], ADA[:, 0, :], ADA[:, 1, :]]
            GC = scratch("GC", [P, 72])
            GG = EX
            sets = []
            for b in range(2):
                q_ = {n: scratch(f"{n}_{b}", [P, T]) for n in ("q", "k", "v", "kb", "d", "l", "t", "n", "a")}
                q_["s"] = scratch(f"s_{b}", [P, P])
                sets.append(q_)
            d_tb = Q.dma("sp", TB2[:, :, :], tab[:, NMAIN + P:NTAB].rearrange("p (n c) -> p n c", c=P), s_lo, 2,
                         fence)
            zu = Q.pool(lambda e: e.memset(UU[:, :, 0:3], 0.0), fence)

            def tb2(name):
                return TB2[:, (TAB[name][0] - NMAIN) // P - 1, :]

            E1 = ZZ[0]

            def ab(m, ps, o):
                be = Q.act(lambda e, ps=ps: e.activation(GG[32:40, :], ps[32:40, :], ACT.Sigmoid), o, fence)
                u = Q.dve(lambda e, ps=ps: e.tensor_scalar(E1[0:8, :], ps[0:8, :], col("dt_bias")[0:8], None,
                                                    ALU.add), o, fence, be)
                i, t, free = tmp()
                a = Q.act(lambda e: e.activation(t[0:8, :], E1[0:8, :], ACT.Abs), u, free)
                a = Q.act(lambda e: e.activation(t[0:8, :], t[0:8, :], ACT.Exp, scale=-1.0), a)
                a = Q.act(lambda e: e.activation(t[0:8, :], t[0:8, :], ACT.Ln, bias=1.0), a)
                n = Q.act(lambda e: e.activation(GC[0:8, 64:65], col("a_log")[0:8], ACT.Exp), fence, d_cols)
                a = Q.dve(lambda e: e.scalar_tensor_tensor(out=t[0:8, :], in0=E1[0:8, :], scalar=0.0,
                                                           in1=t[0:8, :], op0=ALU.max, op1=ALU.add), a)
                a = Q.dve(lambda e: e.tensor_scalar(t[0:8, :], t[0:8, :], GC[0:8, 64:65], -1.0, ALU.mult,
                                                    ALU.mult), a, n)
                for c in range(4):
                    cs = slice(P * c, P * c + P)
                    s = Q.dve(lambda e, cs=cs: e.tensor_tensor_scan(GG[0:8, cs], tb("ones")[0:8, :],
                                                                    t[0:8, cs], 0.0, ALU.mult, ALU.add),
                              a, fence)
                tmp_free[i] = s
                j, p2, free = sml.get()
                for c in range(4):
                    q = Q.pe(lambda e, c=c: e.transpose(p2[:, 8 * c:8 * c + 8], GG[0:8, P * c:P * c + P],
                                                        tb("ident")[0:8, 0:8]), s, free)
                g = Q.dve(lambda e: e.tensor_copy(GC[:, 0:32], p2[:, 0:32]), q, fence)
                sml.done(j, g)
                rows.extend([be, s, g])
                return [be, u]

            rows = []
            dense(1, HH, HL, ready, ab)

            taken = {"u": [zu] * 3, "z": [rows, fence, fence], "all": [fence, fence]}
            gdn_b = Banks(PS[3:8])
            pro_b = Banks(PS[0:3])
            for bk in (gdn_b, pro_b):
                for i in range(len(bk.tiles)):
                    bk.done(i, *(Q.last("act", "dve") + rows))
            raw = {}
            oready = [None] * KT
            DK = P ** -0.5

            def project(h):
                raw[h] = {}
                for n in range(2):
                    j = next_chunk()
                    wh, wl, cut = W.take(j)
                    for c0 in (0, P):
                        r = 2 * n + c0 // P
                        i, ps, free = pro_b.get()
                        for k in range(KT):
                            for part, (a, b) in enumerate(((wh, HH), (wh, HL), (wl, HH))):
                                o = Q.pe(lambda e, ps=ps, a=a, b=b, k=k, c0=c0, part=part: e.matmul(
                                    ps[:, :], a[:, k, c0:c0 + P], b[:, k, :], start=(k == 0 and part == 0),
                                    stop=(k == KT - 1 and part == 2)), free, cut, ready[k])
                            if k < 7:
                                yield
                        if r < 3:
                            t = Q.act(lambda e, r=r, ps=ps: e.activation(UU[:, r, 3:T + 3], ps[:, :],
                                                                         ACT.Copy), o, taken["u"][r])
                        else:
                            t = Q.act(lambda e, ps=ps: e.activation(ZZ[h % 3], ps[:, :], ACT.Copy), o,
                                      taken["z"][h % 3])
                        pro_b.done(i, t)
                        raw[h][r] = t
                        if c0:
                            W.used[j] = o
                        yield
                h_free[0] = o

            def v4(p_):
                return p_[:, :].rearrange("p (c t) -> p c t", c=4)

            def bc(a):
                return a[:, None, :].broadcast_to((P, 4, P))

            def head(h):
                b = h % 2
                S = sets[b]
                QQ, KG, VG, KB = (S[n][:, :] for n in ("q", "k", "v", "kb"))
                DD, LT, TTh, TN, AI = (v4(S[n]) for n in ("d", "l", "t", "n", "a"))
                SG = S["s"]
                G0 = 40 + 8 * b
                before = taken["all"][b]
                dst = (QQ, KG, VG)
                cv = []
                for r in range(3):
                    w0 = 8 * r + h
                    a = Q.dve(lambda e, r=r, w0=w0: e.tensor_scalar(
                        dst[r], UU[:, r, 0:T], col("gconv", w0), None, ALU.mult), raw[h][r], before, zu)
                    for j in range(1, 4):
                        a = Q.dve(lambda e, r=r, j=j, w0=w0: e.scalar_tensor_tensor(
                            out=dst[r], in0=UU[:, r, j:j + T], scalar=col("gconv", 24 * j + w0),
                            in1=dst[r], op0=ALU.mult, op1=ALU.add), a)
                        if j == 1:
                            yield
                    taken["u"][r] = a
                    a = Q.act(lambda e, r=r: e.activation(dst[r], dst[r], ACT.Silu), a)
                    cv.append(a)
                    if r == 2:
                        zs = Q.act(lambda e: e.activation(ZZ[h % 3], ZZ[h % 3], ACT.Silu), raw[h][3])
                    yield
                j, pg, pf = gdn_b.get()
                o = Q.pe(lambda e: e.matmul(pg[:, :], tb("ident")[0:8, h:h + 1].broadcast_to((8, P)),
                                            GG[0:8, :], start=True, stop=True), rows, pf)
                for c in range(4):
                    d = Q.dve(lambda e, c=c: e.tensor_scalar(
                        DD[:, c, :], pg[:, P * c:P * c + P], GC[:, 8 * c + h:8 * c + h + 1], 0.0,
                        ALU.subtract, ALU.min), o, before)
                gl = Q.dve(lambda e: e.tensor_copy(GC[:, G0:G0 + 4], v4(pg)[:, :, 127]), o, before)
                Q.table("natural_log_exp_and_others")
                eg = Q.act(lambda e: e.activation(LT, v4(pg), ACT.Exp), o, before, gl)
                for c in range(4):
                    ek = Q.act(lambda e, c=c: e.activation(TTh[:, c, :], pg[:, P * c:P * c + P], ACT.Exp,
                                                           scale=-1.0, bias=GC[:, G0 + c:G0 + c + 1]), gl,
                               before)
                dd = Q.act(lambda e: e.activation(DD, DD, ACT.Exp), d)
                egl = Q.act(lambda e: e.activation(GC[:, G0 + 4:G0 + 8], GC[:, G0:G0 + 4], ACT.Exp), gl)
                gdn_b.done(j, ek, eg, d, gl)
                yield
                n2, sq, rests = S["a"][:, :], [], []
                for r, n1 in enumerate((S["n"][:, :], KB)):
                    sq.append(Q.act(lambda e, r=r, n1=n1: e.activation(n1, dst[r], ACT.Square), cv[r], before))
                for r, n1 in enumerate((S["n"][:, :], KB)):
                    j, ps, pf = gdn_b.get(hold=True)
                    o = Q.pe(lambda e, ps=ps, n1=n1: e.matmul(ps[:, :], tb("ones"), n1, start=True, stop=True),
                             sq[r], pf)
                    rests.append((j, ps, n1, o))
                yield
                nrm = [before]
                for r, (j, ps, n1, o) in enumerate(rests):
                    rest = rsqrt_parts(n1, n2, ps[:, :], o, 1.0, 1e-6, nrm)
                    yield
                    y, a = rest()
                    gdn_b.done(j, y)
                    a = Q.dve(lambda e, r=r, n1=n1: e.scalar_tensor_tensor(
                        out=dst[r], in0=dst[r], scalar=DK if r == 0 else 1.0, in1=n1, op0=ALU.mult,
                        op1=ALU.mult), a)
                    nrm.append(a)
                yield
                di = Q.pool(lambda e: e.tensor_tensor(AI, DD, bc(tb("supi")), ALU.mult), dd, nrm)
                ds = Q.pool(lambda e: e.tensor_tensor(DD, DD, bc(tb("sup")), ALU.mult), di)
                j, pb_, pf = gdn_b.get()
                o = Q.pe(lambda e: e.matmul(pb_[:, :], tb("ident")[32:40, 32 + h:33 + h].broadcast_to((8, P)),
                                            GG[32:40, :], start=True, stop=True), rows, pf)
                kb = Q.dve(lambda e: e.tensor_tensor(KB, KG, pb_[:, :], ALU.mult), o, nrm)
                vb = Q.dve(lambda e: e.tensor_tensor(VG, VG, pb_[:, :], ALU.mult), cv)
                gdn_b.done(j, vb)
                yield
                j1, p1, pf1 = gdn_b.get()
                for c in range(4):
                    cs = slice(P * c, P * c + P)
                    o1 = Q.pe(lambda e, cs=cs: e.matmul(p1[:, cs], KG[:, cs], KB[:, cs], start=True,
                                                        stop=True), kb, pf1)
                j2, p2, pf2 = gdn_b.get()
                for c in range(4):
                    cs = slice(P * c, P * c + P)
                    o2 = Q.pe(lambda e, cs=cs: e.matmul(p2[:, cs], KG[:, cs], QQ[:, cs], start=True,
                                                        stop=True), nrm, pf2)
                EG, EK = S["l"][:, :], S["t"][:, :]
                kd = Q.dve(lambda e: e.tensor_tensor(KG, KG, EK, ALU.mult), ek, o1, o2)
                qd = Q.dve(lambda e: e.tensor_tensor(QQ, QQ, EG, ALU.mult), eg, o2)
                ke = Q.dve(lambda e: e.tensor_tensor(KB, KB, EG, ALU.mult), eg, o1)
                l = Q.dve(lambda e: e.scalar_tensor_tensor(out=LT, in0=v4(p1), scalar=-1.0, in1=DD,
                                                           op0=ALU.mult, op1=ALU.mult), o1, ds, ke, qd)
                gdn_b.done(j1, l)
                t0 = Q.dve(lambda e: e.tensor_tensor(TTh, LT, bc(tb2("upp0")), ALU.mult), l, d_tb, kd)
                t0 = Q.dve(lambda e: e.tensor_tensor(TTh, TTh, bc(tb("ident")), ALU.add), t0)
                ai = Q.dve(lambda e: e.tensor_tensor(AI, v4(p2), AI, ALU.mult), o2, di)
                gdn_b.done(j2, ai)
                yield
                j, ps, pf = gdn_b.get()
                for c in range(4):
                    cs = slice(P * c, P * c + P)
                    o = Q.pe(lambda e, cs=cs, ps=ps: e.transpose(ps[:, cs], KG[:, cs], tb("ident")), kd, pf)
                kt = Q.act(lambda e, ps=ps: e.activation(DD, v4(ps), ACT.Copy), o, l)
                gdn_b.done(j, kt)
                UN, tto = v4(S["k"]), None
                for v in inverse(LT, TTh, TN, UN, tb2, 7, gdn_b, [t0, o]):
                    if v:
                        tto = v
                    yield
                inv = Q.last("pe", "dve")
                XK, XV, KD, WT, US = TN, UN, DD, v4(S["kb"]), v4(S["v"])
                tk = [kt]
                for src, dstt, w_ in ((VG, XV, vb), (KB, XK, ke)):
                    j, ps, pf = gdn_b.get()
                    for c in range(4):
                        cs = slice(P * c, P * c + P)
                        o = Q.pe(lambda e, cs=cs, src=src, ps=ps: e.transpose(ps[:, cs], src[:, cs],
                                                                              tb("ident")), w_, pf)
                    a = Q.act(lambda e, ps=ps, dstt=dstt: e.activation(dstt, v4(ps), ACT.Copy), o, inv)
                    gdn_b.done(j, a)
                    tk.append(a)
                yield
                j, ps, pf = gdn_b.get()
                for c in range(4):
                    o = Q.pe(lambda e, c=c, ps=ps: e.matmul(ps[:, P * c:P * c + P], TTh[:, c, :],
                                                            XV[:, c, :], start=True, stop=True), tto, tk, pf)
                us = Q.dve(lambda e, ps=ps: e.tensor_copy(US, v4(ps)), o, tk)
                gdn_b.done(j, us)
                j, ps, pf = gdn_b.get()
                for c in range(1, 4):
                    o = Q.pe(lambda e, c=c, ps=ps: e.matmul(ps[:, P * c:P * c + P], XK[:, c, :],
                                                            TTh[:, c, :], start=True, stop=True), pf)
                wt = Q.act(lambda e, ps=ps: e.activation(WT[:, 1:4, :], v4(ps)[:, 1:4, :], ACT.Copy), o, tk)
                gdn_b.done(j, wt)
                yield
                jo, po, pfo = gdn_b.get(hold=True)
                s = None
                for c in range(4):
                    cs = slice(P * c, P * c + P)
                    vn = us
                    if c:
                        j, ps, pf = gdn_b.get()
                        o = Q.pe(lambda e, c=c, ps=ps: e.matmul(ps[:, 0:P], WT[:, c, :], SG[:, :],
                                                                start=True, stop=True), wt, s, pf)
                        vn = Q.dve(lambda e, c=c, ps=ps: e.tensor_tensor(US[:, c, :], US[:, c, :],
                                                                         ps[:, 0:P], ALU.subtract), o)
                        gdn_b.done(j, vn)
                        Q.pe(lambda e, cs=cs: e.matmul(po[:, cs], SG[:, :], QQ[:, cs], start=True,
                                                       stop=False), qd, s, pfo)
                        yield
                    if c < 3:
                        j, ps, pf = gdn_b.get()
                        o = Q.pe(lambda e, c=c, ps=ps: e.matmul(ps[:, 0:P], KD[:, c, :], US[:, c, :],
                                                                start=True, stop=True), vn, tk, pf)
                    oo = Q.pe(lambda e, cs=cs, c=c: e.matmul(po[:, cs], US[:, c, :], AI[:, c, :],
                                                             start=(c == 0), stop=True), vn, ai, pfo)
                    if c < 3:
                        if c == 0:
                            s = Q.dve(lambda e, ps=ps: e.tensor_copy(SG[:, :], ps[:, 0:P]), o, before)
                        else:
                            s = Q.dve(lambda e, c=c, ps=ps: e.scalar_tensor_tensor(
                                out=SG[:, :], in0=SG[:, :], scalar=GC[:, G0 + 4 + c:G0 + 5 + c],
                                in1=ps[:, 0:P], op0=ALU.mult, op1=ALU.add), o, egl, oo)
                        gdn_b.done(j, s)
                        yield
                i, t, free = tmp()
                a = Q.act(lambda e, t=t: e.activation(t, po[:, :], ACT.Square), oo, free)
                oc = Q.dve(lambda e: e.tensor_scalar(QQ, po[:, :], col("o_gain"), None, ALU.mult), oo, a)
                gdn_b.done(jo, a, oc)
                oz = Q.dve(lambda e: e.tensor_tensor(QQ, QQ, ZZ[h % 3], ALU.mult), oc, zs)
                taken["z"][h % 3] = oz
                j, ps, pf = gdn_b.get(hold=True)
                o = Q.pe(lambda e, t=t, ps=ps: e.matmul(ps[:, :], tb("ones"), t, start=True, stop=True), a,
                         pf)
                i2, t2, f2 = tmp()
                rest = rsqrt_parts(t, t2, ps[:, :], o, 1.0 / P, 1e-6, f2)
                yield
                y, a = rest()
                gdn_b.done(j, y)
                tmp_free[i2] = a
                a = Q.dve(lambda e, t=t: e.tensor_tensor(OF[:, h, :], t, QQ, ALU.mult), a, oz, fence)
                tmp_free[i] = oready[h] = a
                taken["all"][b] = Q.last("dve", "act", "pool", "pe")
                yield

            W.gentle = True
            for _ in project(0):
                pass
            HALF = 21
            old = iter(())
            for h in range(9):
                new = head(h) if h < 8 else iter(())
                pro = project(h + 1) if h < 7 else iter(())
                for step in range(HALF):
                    next(old, None)
                    next(pro, None)
                    next(new, None)
                    next(pro, None)
                    W.settle(1)
                for _ in old:
                    pass
                for _ in pro:
                    pass
                old = new
            W.settle()
            W.gentle = False
            end = Q.last("act", "dve", "pe")
            for bk in (big, sml):
                for i in range(4):
                    bk.done(i, *end)
            hready = [split_into(HH[:, k, :], HL[:, k, :], OF[:, k, :], oready[k], h_free[0])
                      for k in range(KT)]
            h_free[0] = last = dense(4, HH, HL, hready, residual(None, None, True))
            for m in range(16):
                g_free[m] = Q.last("pe", "dve", "act", "pool")

        def sb_mixer():
            rstd = rms()
            KS = place("KS", [P, 8, T], F32, ar_at)
            VT = place("VT", [P, 4, D], F32, ar_at + 16384)
            QS = place("QS", [P, 8, T], F32, ar_at + 32768)
            fence = Q.last("pe", "act", "dve", "pool")
            SCALE = P ** -0.5

            def heads(dst, gname, ready_to):
                held = []

                def flush():
                    while held:
                        held.pop(0)()

                def consume(m, ps, o):
                    flush()
                    i = m % 2
                    t = SQ[:, i, :]
                    a = Q.act(lambda e, ps=ps: e.activation(t, ps[:, :], ACT.Square), o, h_free_t[i], fence)
                    g = Q.dve(lambda e, ps=ps: e.tensor_scalar(dst[:, m, :], ps[:, :], col(gname), None, ALU.mult),
                              o, fence, a)
                    held.append(lambda: norm(m, i, t, a, g))
                    return [a, g]

                def norm(m, i, t, a, g):
                    j, p2, pf = sml.get()
                    q = Q.pe(lambda e: e.matmul(p2[:, :], tb("ones"), t, start=True, stop=True), a, pf)
                    i2, t2, f2 = tmp()
                    r, b = rsqrt(t, t2, p2[:, :], q, 1.0 / P, 1e-6, f2)
                    sml.done(j, r)
                    tmp_free[i2] = b
                    b = Q.dve(lambda e: e.tensor_tensor(dst[:, m, :], dst[:, m, :], t, ALU.mult), b, g)
                    h_free_t[i] = b
                    ready_to[m] = b
                return consume, flush

            SQ = place("SQ", [P, 2, T], F32, ar_at + 49152)
            h_free_t = [None, None]

            kr, qr, vr = [None] * 8, [None] * 8, [None] * 4
            ready = norm_split(lambda k: col("kv_norm", k), d_cols, None, rstd)
            ck, fk = heads(KS, "k_gain", kr)
            dense(4, HH, HL, ready, ck)
            for n in range(4):
                j = next_chunk()
                wh, wl, cut = W.take(j)
                for tbk in range(4):
                    i, ps, free = big.get()
                    ts = slice(P * tbk, P * tbk + P)
                    if tbk == 1:
                        fk()
                    for k in range(KT):
                        for part, (a, b) in enumerate(((wh, HH), (wh, HL), (wl, HH))):
                            o = Q.pe(lambda e, ps=ps, a=a, b=b, k=k, ts=ts, part=part: e.matmul(
                                ps[:, 0:256], b[:, k, ts], a[:, k, :], start=(k == 0 and part == 0),
                                stop=(k == KT - 1 and part == 2)), free, cut, ready[k])
                    v = Q.act(lambda e, ps=ps, tbk=tbk, n=n: e.activation(
                        VT[:, tbk, 256 * n:256 * n + 256], ps[:, 0:256], ACT.Copy), o, fence)
                    big.done(i, v)
                vr[n] = v
                W.used[j] = o
            h_free[0] = o
            ready = norm_split(lambda k: col("attn_norm", 8 + k), d_cols, None, rstd)
            W.limit = sched.index(("so", 0)) + 3
            cq, fq = heads(QS, "q_gain", qr)
            h_free[0] = dense(4, HH, HL, ready, cq)
            fq()
            W.cut(W.where[sched.index(("so", 0))] + 2)
            fence = Q.last("pe", "act", "dve", "pool")
            LFT = [place(f"LF{b}", [P, 1280], F32, (st_at, ar_at + 49152)[b % 2] + 5120 * (b // 2))
                   for b in range(4)]
            ZST = [place(f"ZS{b}", [P, T], F32, (st_at, ar_at + 49152)[b % 2] + 10240 + 2048 * (b // 2))
                   for b in range(4)]
            ATT = [place(f"AT{b}", [P, T], F32, (st_at, ar_at + 49152)[b % 2] + 14336 + 2048 * (b // 2))
                   for b in range(4)]
            Q.table("natural_log_exp_and_others")
            off = [0, 512, 896, 1152]
            hready = [None] * KT
            lf_free, zs_free, at_free = [None] * 4, [None] * 4, [None] * 4
            zb, rb, ob = Banks(PS[0:2]), Banks(PS[2:4]), Banks(PS[4:8])
            for bk in (zb, rb, ob):
                for i in range(len(bk.tiles)):
                    bk.done(i, *Q.last("act", "dve"))

            def attend(h):
                b = h % 4
                LF, ZS, AT = LFT[b], ZST[b], ATT[b]
                jo, po, pfo = ob.get()
                lf = {}
                def scores(j):
                    w_ = T - P * j
                    L, Z = LF[:, off[j]:off[j] + w_], ZS[:, 0:w_]
                    i, ps, pf = zb.get()
                    o = Q.pe(lambda e, ps=ps: e.matmul(ps[:, 0:w_], KS[:, h, P * j:P * j + P], QS[:, h, P * j:T],
                                                start=True, stop=True), kr, qr, pf)
                    z = Q.act(lambda e, ps=ps: e.activation(Z, ps[:, 0:w_], ACT.Identity, scale=SCALE), o,
                              zs_free[b], fence)
                    a = Q.act(lambda e, ps=ps: e.activation(L, ps[:, 0:w_], ACT.Abs, scale=SCALE), o, lf_free[b],
                              fence)
                    zb.done(i, z, a)
                    a = Q.act(lambda e: e.activation(L, L, ACT.Exp, scale=-1.0), a)
                    a = Q.act(lambda e: e.activation(L, L, ACT.Ln, bias=1.0), a)
                    a = Q.dve(lambda e: e.scalar_tensor_tensor(out=L, in0=Z, scalar=0.0, in1=L, op0=ALU.max,
                                                               op1=ALU.add), a, z)
                    lf[j] = Q.dve(lambda e: e.tensor_tensor(L[:, 0:P], L[:, 0:P], tb("sup"), ALU.mult), a)
                    zm[j] = Q.dve(lambda e: e.tensor_tensor(Z[:, 0:P], Z[:, 0:P], tb("sup"), ALU.mult), a)

                def weights(j):
                    w_ = T - P * j
                    Z, Aw = ZS[:, 0:w_], AT[:, 0:w_]
                    i, pr, pf = rb.get()
                    for j2 in range(j, 4):
                        w2 = T - P * j2
                        o = Q.pe(lambda e, j2=j2, w2=w2: e.matmul(
                            pr[:, w_ - w2:w_], tb("tri" if j2 == j else "ones"),
                            LF[:, off[j2]:off[j2] + w2], start=(j2 == j), stop=(j2 == 3)), lf[j2], pf)
                    d = Q.dve(lambda e: e.scalar_tensor_tensor(
                        out=Aw, in0=pr[:, 0:w_], scalar=-1.0, in1=Z, op0=ALU.mult, op1=ALU.add), o, zm[j],
                        at_free[b])
                    rb.done(i, d)
                    zs_free[b] = d
                    d = Q.act(lambda e: e.activation(Aw, Aw, ACT.Exp), d)
                    return o, Q.dve(lambda e: e.tensor_tensor(Aw[:, 0:P], Aw[:, 0:P], tb("sup"), ALU.mult),
                                    d)

                zm = {}
                scores(3)
                yield
                for j in (3, 2, 1, 0):
                    lo_, d = weights(j)
                    if j:
                        scores(j - 1)
                    yield
                    o = Q.pe(lambda e, j=j: e.matmul(
                        po[:, P * j:T], VT[:, j, P * h:P * h + P], AT[:, 0:T - P * j], start=(j == 3),
                        stop=(j == 0), skip_group_check=True), d, vr, pfo)
                    at_free[b] = o
                lf_free[b] = lo_
                hi = Q.act(lambda e: e.activation(HH[:, h, :], po[:, :], ACT.Copy), o, h_free[0])
                lo = Q.dve(lambda e: e.tensor_tensor(HL[:, h, :], po[:, :], HH[:, h, :].bitcast(F32),
                                                     ALU.subtract), hi)
                hready[h] = [hi, lo]
                ob.done(jo, hi, lo)

            for h in range(0, 8, 4):
                interleave(*[attend(h + i) for i in range(4)])
            W.fence = Q.last("pe", "act", "dve", "pool")
            W.limit = len(sched)
            end = Q.last("act", "dve")
            for bk in (big, sml):
                for i in range(4):
                    bk.done(i, *end)
            h_free[0] = dense(4, HH, HL, hready, residual(None, None, True))
            for m in range(16):
                g_free[m] = Q.last("pe", "dve", "act", "pool")

        def whole():
            conv_mixer()
            if stop == "conv":
                return
            mlp(0)
            if stop == "mlp0":
                return
            rwkv_mixer()
            if stop == "rwkv":
                return
            mlp(1)
            if stop == "mlp1":
                return
            gdn_mixer()
            if stop in ("fin", "gdn"):
                return
            swiglu(0)
            if stop == "ffn0":
                return
            sb_mixer()
            if stop == "sb":
                return
            swiglu(1)

        whole()
        finish()
        Q.number()
        block = ctx.enter_context(nc.Block())

        @block.sync
        def _(e):
            Q.emit("sp", e)
            e.wait_ge(s_out, 16)

        @block.scalar
        def _(e):
            Q.emit("act", e)

        @block.vector
        def _(e):
            Q.emit("dve", e)

        @block.gpsimd
        def _(e):
            Q.emit("pool", e)

        @block.tensor
        def _(e):
            Q.emit("pe", e)


def layout(inputs):
    def vec(a):
        return np.asarray(a).reshape(-1, P).T

    def chunks(a, c=256):
        a = np.asarray(a)
        k, n = a.shape
        return np.ascontiguousarray(a.reshape(k // P, P, n // c, c).transpose(2, 1, 0, 3)).reshape(n // c, P, -1)

    def rowpad(a):
        z = np.zeros((P, 1), np.float32)
        z[:a.shape[0], 0] = a
        return z

    g = {k: np.asarray(v) for k, v in inputs.items()}
    cols = {
        "c": vec(g["c"]), "norm_g": vec(g["norm_g"]), "final_g": vec(g["final_g"]), "ada_b": vec(g["ada_b"]),
        "conv_w": vec(g["conv_w"]), "mu": vec(g["rw_mu"]), "w0": vec(g["rw_w0"]), "a0": vec(g["rw_a0"]),
        "k_k": vec(g["rw_k_k"]), "k_a": vec(g["rw_k_a"]), "r_k": vec(g["rw_r_k"]), "ln_w": vec(g["rw_ln_w"]),
        "ln_b": vec(g["rw_ln_b"]), "attn_norm": vec(g["attn_norm_2"]), "ffn_norm": vec(g["ffn_norm_2"]),
        "kv_norm": vec(g["kv_norm_2"]), "gconv": vec(g["gdn_conv_w_2"]), "o_gain": vec(g["gdn_o_gain_2"]),
        "k_gain": vec(g["k_gain_2"]), "q_gain": vec(g["sb_q_gain_2"]), "a_log": rowpad(g["gdn_a_log_2"][0]),
        "dt_bias": rowpad(g["gdn_dt_bias_2"][0]),
    }
    packed = np.concatenate([cols[n] for n in COLS], axis=1).astype(np.float32, copy=False)
    ada = g["ada_w"].reshape(2, 2, 4, P, 12, 512).transpose(0, 4, 1, 3, 2, 5).reshape(48, P, 2048)

    def cat(*a):
        return np.concatenate(a, axis=0)

    cin = g["conv_w_in"][0]
    parts = []
    for q in range(4):
        a, b = 256 * q, 256 * q + P
        for f in (a, b):
            parts += [cin[:, 1024 + f:1024 + f + P], cin[:, 2048 + f:2048 + f + P]]
        parts.append(cin[:, a:a + 256])
    rkv = g["rw_w_rkv"][0]
    gin = g["gdn_w_in_2"][0]
    n = QKVZ = 4096
    gab = np.concatenate([gin[:, n + 8:n + 16], gin[:, 0:24], gin[:, n:n + 8], gin[:, 0:88]], axis=1)
    heads = []
    for h in range(8):
        heads += [gin[:, j * 1024 + h * P:j * 1024 + h * P + P] for j in range(4)]

    def gu(a):
        f = a.shape[1] // 2
        return chunks(np.concatenate([a[:, s + i * P:s + i * P + P] for i in range(22) for s in (0, f)], axis=1))

    def m2(a, n):
        return cat(*[chunks(a[i * n * P:(i + 1) * n * P], P) for i in range(2)])

    w = {
        "cin": chunks(np.concatenate(parts, axis=1)), "cout": chunks(g["conv_w_out"][0]),
        "m1": cat(*[chunks(a) for a in g["mlp_w1"]]), "m2": cat(*[m2(a, 16) for a in g["mlp_w2"]]),
        "lwa": chunks(np.concatenate([g["rw_w1"][0], g["rw_a1"][0]], axis=1), 128),
        "lg": chunks(g["rw_g1"][0], 160),
        "rkv": cat(*[chunks(a) for a in rkv]), "wo": chunks(g["rw_w_o"][0]),
        "gab": chunks(gab, 128), "gin": chunks(np.concatenate(heads, axis=1)), "gout": chunks(g["gdn_w_out_2"][0]),
        "kv": chunks(g["w_kv_2"]), "sq": chunks(g["sb_w_q_2"][0]), "so": chunks(g["sb_w_out_2"][0]),
        "ada": ada, "gu": cat(*[gu(a) for a in g["ffn_w_gu_2"]]), "dn": cat(*[m2(a, 11) for a in g["ffn_w_down_2"]]),
    }
    g2 = g["rw_g2"][0]
    lo2 = np.stack([cat(g["rw_w2"][0], g["rw_a2"][0]), g2[0:128], cat(g2[64:160], g2[128:160])], axis=1)
    return {
        "x": g["x"][0].T.reshape(KT, P, T).transpose(1, 0, 2), "cols": packed, "tab": tables(),
        "lo2": lo2, **{"w_" + k: v for k, v in w.items()},
    }


def kernel(**inputs):
    import concourse.bacc as bacc
    from concourse.bass_utils import run_bass_kernel_spmd

    nc = bacc.Bacc("TRN2", target_bir_lowering=False, num_devices=1)
    arrays = {k: np.ascontiguousarray(v) for k, v in layout(inputs).items()}
    t = {k: nc.dram_tensor(k, v.shape, F32, kind="ExternalInput").ap() for k, v in arrays.items()}
    out = nc.dram_tensor("out", (P, KT, T), F32, kind="ExternalOutput").ap()
    build(nc, t["x"], t["cols"], t["tab"], {k: t["w_" + k] for k in STREAM}, t["lo2"], out)
    r = run_bass_kernel_spmd(nc, [arrays], core_ids=[0])
    y = r.results[0]["out"]
    return np.ascontiguousarray(y.transpose(1, 0, 2).reshape(D, T).T).reshape(1, T, D)
```
